# Optimizing a Trainium2 kernel written in Bass

```python
import math
import jax, jax.numpy as jnp
from jax import lax
import numpy as np

D_MODEL = 1024
BATCH = 1
SEQ = 256
DEPTH = 4

HEAD_DIM = 64
N_HEADS = D_MODEL // HEAD_DIM
D_FF = 2816
NORM_EPS = 1e-6
N_MIXERS = 3

REL_BUCKETS = 32
REL_MAX_DIST = 1024

QBLK = 128

A_KV_HEADS = 2
A_WINDOW = 128

B_KV_GROUPS = 4
CMP_LEN = 32
CMP_STRIDE = 16
CMP_HIDDEN = 256
SLC_BLK = 64
SLC_TOPK = 16
B_WINDOW = 512
B_QCHUNK = 128

MOBA_BLK = 256
MOBA_TOPK = 3
MOBA_QCHUNK = 64

NEG = -1e30
TINY = 1e-30

A_IN = N_HEADS * HEAD_DIM + 2 * A_KV_HEADS * HEAD_DIM
B_IN = N_HEADS * HEAD_DIM + 6 * B_KV_GROUPS * HEAD_DIM + 3 * N_HEADS
C_IN = 3 * N_HEADS * HEAD_DIM

N_A_LAYERS = (DEPTH + 2) // 3
N_B_LAYERS = (DEPTH + 1) // 3
N_C_LAYERS = DEPTH // 3


def rms_norm(x, g):
    xf = x.astype(jnp.float32)
    y = xf * lax.rsqrt(jnp.mean(xf * xf, axis=-1, keepdims=True) + NORM_EPS)
    return (y * g.astype(jnp.float32)).astype(x.dtype)

def swiglu(h, w_in, w_out):
    gate, up = jnp.split(h @ w_in, 2, axis=-1)
    return (jax.nn.silu(gate) * up) @ w_out

def rel_bucket(dist):
    dist = jnp.maximum(dist, 0)
    exact = REL_BUCKETS // 2
    d = jnp.maximum(dist, 1).astype(jnp.float32)
    log_b = exact + (jnp.log(d / exact) / math.log(REL_MAX_DIST / exact)
                     * (REL_BUCKETS - exact)).astype(jnp.int32)
    return jnp.where(dist < exact, dist, jnp.minimum(log_b, REL_BUCKETS - 1))

def masked_softmax(s, ok, sink=None):
    s = jnp.where(ok, s, NEG)
    m = jnp.max(s, axis=-1, keepdims=True)
    if sink is not None:
        m = jnp.maximum(m, sink)
    e = jnp.where(ok, jnp.exp(s - m), 0.0)
    denom = jnp.sum(e, axis=-1, keepdims=True)
    if sink is not None:
        denom = denom + jnp.exp(sink - m)
    return e / jnp.maximum(denom, TINY)

def banded_attention(q, k, v, rel_table, window, sinks=None):
    B, S, H, dh = q.shape
    G = k.shape[2]
    R = H // G
    n_prev = -(-(window - 1) // QBLK)
    pad = n_prev * QBLK
    slab = pad + QBLK
    kp = jnp.pad(k, ((0, 0), (pad, 0), (0, 0), (0, 0)))
    vp = jnp.pad(v, ((0, 0), (pad, 0), (0, 0), (0, 0)))
    n_blk = S // QBLK
    qb = q.reshape(B, n_blk, QBLK, G, R, dh).transpose(1, 0, 2, 3, 4, 5)
    qi = jnp.arange(QBLK)[:, None]
    kj = jnp.arange(slab)[None, :]
    dist = pad + qi - kj
    in_band = (dist >= 0) & (dist < window)
    bias = rel_table.astype(jnp.float32)[rel_bucket(dist)]
    bias = bias.reshape(QBLK, slab, G, R).transpose(2, 3, 0, 1)
    sink = None if sinks is None else sinks.astype(jnp.float32).reshape(G, R, 1, 1)
    scale = dh ** -0.5

    def block(args):
        n, q_n = args
        start = n * QBLK
        k_n = lax.dynamic_slice_in_dim(kp, start, slab, axis=1)
        v_n = lax.dynamic_slice_in_dim(vp, start, slab, axis=1)
        s = jnp.einsum("bqgrd,bkgd->bgrqk", q_n, k_n).astype(jnp.float32) * scale + bias
        ok = in_band & (start - pad + kj >= 0)
        p = masked_softmax(s, ok, sink)
        o = jnp.einsum("bgrqk,bkgd->bqgrd", p.astype(v.dtype), v_n)
        return o.reshape(B, QBLK, H, dh)

    out = lax.map(block, (jnp.arange(n_blk), qb))
    return out.transpose(1, 0, 2, 3, 4).reshape(B, S, H, dh)

def sliding_sink_attention(h, w_in, w_out, sinks, rel_table):
    B, S, _ = h.shape
    qw, kw = N_HEADS * HEAD_DIM, A_KV_HEADS * HEAD_DIM
    q, k, v = jnp.split(h @ w_in, [qw, qw + kw], axis=-1)
    q = q.reshape(B, S, N_HEADS, HEAD_DIM)
    k = k.reshape(B, S, A_KV_HEADS, HEAD_DIM)
    v = v.reshape(B, S, A_KV_HEADS, HEAD_DIM)
    o = banded_attention(q, k, v, rel_table, A_WINDOW, sinks)
    return o.reshape(B, S, -1) @ w_out

def compress_kv(kv, pos, w1, w2):
    B, S, G, dh = kv.shape
    n_cmp = (S - CMP_LEN) // CMP_STRIDE + 1
    idx = jnp.arange(n_cmp)[:, None] * CMP_STRIDE + jnp.arange(CMP_LEN)[None, :]
    blocks = kv[:, idx] + pos[:, None, :]
    flat = blocks.transpose(0, 1, 3, 2, 4).reshape(B, n_cmp, G, CMP_LEN * dh)
    return jax.nn.gelu(flat @ w1) @ w2

def selected_block_attention(q, k, v, sel_idx, rel_table):
    B, S, G, R, dh = q.shape
    n_sel = sel_idx.shape[-1]
    n_slc = S // SLC_BLK
    kb = k.reshape(B, n_slc, SLC_BLK, G, dh).transpose(0, 3, 1, 2, 4)
    vb = v.reshape(B, n_slc, SLC_BLK, G, dh).transpose(0, 3, 1, 2, 4)
    table_g = rel_table.astype(jnp.float32).reshape(REL_BUCKETS, G, R).transpose(1, 0, 2)
    g_ix = jnp.arange(G)[:, None, None]
    n_q = S // B_QCHUNK
    n_keys = n_sel * SLC_BLK
    scale = dh ** -0.5

    def chunk(i):
        b, c = i // n_q, i % n_q
        start = c * B_QCHUNK
        q_c = lax.dynamic_slice_in_dim(q[b], start, B_QCHUNK, axis=0)
        idx = lax.dynamic_slice_in_dim(sel_idx[b], start, B_QCHUNK, axis=1)
        k_sel = kb[b][g_ix, idx].reshape(G, B_QCHUNK, n_keys, dh)
        v_sel = vb[b][g_ix, idx].reshape(G, B_QCHUNK, n_keys, dh)
        pos = (idx[..., None] * SLC_BLK + jnp.arange(SLC_BLK)).reshape(G, B_QCHUNK, n_keys)
        t = start + jnp.arange(B_QCHUNK)
        dist = t[None, :, None] - pos
        bias = table_g[g_ix, rel_bucket(dist)].transpose(0, 3, 1, 2)
        s = jnp.einsum("qgrd,gqkd->grqk", q_c, k_sel).astype(jnp.float32) * scale + bias
        p = masked_softmax(s, (dist >= 0)[:, None])
        o = jnp.einsum("grqk,gqkd->qgrd", p.astype(v.dtype), v_sel)
        return o.reshape(B_QCHUNK, G * R, dh)

    out = lax.map(chunk, jnp.arange(B * n_q))
    return out.reshape(B, S, G * R, dh)

def nsa_attention(h, w_in, w_out, cmp_pos, cmp_w1, cmp_w2, rel_table):
    B, S, _ = h.shape
    G, R, dh = B_KV_GROUPS, N_HEADS // B_KV_GROUPS, HEAD_DIM
    kvw = G * dh
    splits = np.cumsum([N_HEADS * dh] + [kvw] * 6).tolist()
    q, kc, vc, ks, vs, kw, vw, gate = jnp.split(h @ w_in, splits, axis=-1)
    q = q.reshape(B, S, G, R, dh)
    to_kv = lambda a: a.reshape(B, S, G, dh)
    scale = dh ** -0.5
    t = jnp.arange(S)

    kc_b = compress_kv(to_kv(kc), cmp_pos[0], cmp_w1[0], cmp_w2[0])
    vc_b = compress_kv(to_kv(vc), cmp_pos[1], cmp_w1[1], cmp_w2[1])
    n_cmp = kc_b.shape[1]
    cmp_end = jnp.arange(n_cmp) * CMP_STRIDE + CMP_LEN - 1
    s_cmp = jnp.einsum("bsgrd,bngd->bgrsn", q, kc_b).astype(jnp.float32) * scale
    p_cmp = masked_softmax(s_cmp, cmp_end[None, :] <= t[:, None])
    o_cmp = jnp.einsum("bgrsn,bngd->bsgrd", p_cmp.astype(vc_b.dtype), vc_b)

    n_slc = S // SLC_BLK
    n_sel = min(SLC_TOPK, n_slc)
    c_start = np.arange(n_cmp)[:, None] * CMP_STRIDE
    s_start = np.arange(n_slc)[None, :] * SLC_BLK
    overlap = ((c_start < s_start + SLC_BLK) & (c_start + CMP_LEN > s_start)).astype(np.float32)
    imp = jnp.einsum("bgrsn,nj->bgsj", p_cmp, jnp.asarray(overlap))
    cur = (t // SLC_BLK)[:, None]
    j = jnp.arange(n_slc)[None, :]
    forced = (j == 0) | (j == cur) | (j == cur - 1)
    imp = jnp.where(j > cur, NEG, jnp.where(forced, -NEG, imp))
    _, sel_idx = lax.top_k(imp, n_sel)
    o_slc = selected_block_attention(q, to_kv(ks), to_kv(vs), sel_idx, rel_table)

    o_win = banded_attention(q.reshape(B, S, N_HEADS, dh), to_kv(kw), to_kv(vw),
                             rel_table, B_WINDOW)

    g = jax.nn.sigmoid(gate.astype(jnp.float32)).reshape(B, S, N_HEADS, 3).astype(o_win.dtype)
    o = (g[..., 0:1] * o_cmp.reshape(B, S, N_HEADS, dh)
         + g[..., 1:2] * o_slc + g[..., 2:3] * o_win)
    return o.reshape(B, S, -1) @ w_out

def moba_attention(h, w_in, w_out, rel_table):
    B, S, _ = h.shape
    H, dh = N_HEADS, HEAD_DIM
    q, k, v = jnp.split(h @ w_in, 3, axis=-1)
    q = q.reshape(B, S, H, dh)
    k = k.reshape(B, S, H, dh)
    v = v.reshape(B, S, H, dh)
    n_blk = -(-S // MOBA_BLK)
    s_pad = n_blk * MOBA_BLK
    kb = jnp.pad(k, ((0, 0), (0, s_pad - S), (0, 0), (0, 0))).reshape(B, n_blk, MOBA_BLK, H, dh)
    vb = jnp.pad(v, ((0, 0), (0, s_pad - S), (0, 0), (0, 0))).reshape(B, n_blk, MOBA_BLK, H, dh)
    n_top = min(MOBA_TOPK, n_blk - 1)
    table = rel_table.astype(jnp.float32)
    table_h = table.T
    scale = dh ** -0.5
    t = jnp.arange(S)
    if n_top > 0:
        k_mean = jnp.mean(kb.astype(jnp.float32), axis=2).astype(q.dtype)
        gate = jnp.einsum("bshd,bnhd->bhsn", q, k_mean).astype(jnp.float32)
        past = jnp.arange(n_blk)[None, :] < (t // MOBA_BLK)[:, None]
        _, sel = lax.top_k(jnp.where(past, gate, NEG), n_top)
        kbh = kb.transpose(0, 3, 1, 2, 4)
        vbh = vb.transpose(0, 3, 1, 2, 4)
    h_ix = jnp.arange(H)[:, None, None]
    n_q = S // MOBA_QCHUNK

    def chunk(i):
        b, c = i // n_q, i % n_q
        start = c * MOBA_QCHUNK
        q_c = lax.dynamic_slice_in_dim(q[b], start, MOBA_QCHUNK, axis=0)
        tq = start + jnp.arange(MOBA_QCHUNK)
        own = start // MOBA_BLK
        k_own = lax.dynamic_index_in_dim(kb[b], own, axis=0, keepdims=False)
        v_own = lax.dynamic_index_in_dim(vb[b], own, axis=0, keepdims=False)
        d_own = tq[:, None] - (own * MOBA_BLK + jnp.arange(MOBA_BLK))[None, :]
        s_own = (jnp.einsum("qhd,khd->hqk", q_c, k_own).astype(jnp.float32) * scale
                 + table[rel_bucket(d_own)].transpose(2, 0, 1))
        ok_own = jnp.broadcast_to(d_own >= 0, s_own.shape)
        if n_top == 0:
            p = masked_softmax(s_own, ok_own)
            return jnp.einsum("hqk,khd->qhd", p.astype(v.dtype), v_own)
        idx = lax.dynamic_slice_in_dim(sel[b], start, MOBA_QCHUNK, axis=1)
        n_keys = n_top * MOBA_BLK
        k_sel = kbh[b][h_ix, idx].reshape(H, MOBA_QCHUNK, n_keys, dh)
        v_sel = vbh[b][h_ix, idx].reshape(H, MOBA_QCHUNK, n_keys, dh)
        pos = (idx[..., None] * MOBA_BLK + jnp.arange(MOBA_BLK)).reshape(H, MOBA_QCHUNK, n_keys)
        d_sel = tq[None, :, None] - pos
        s_sel = (jnp.einsum("qhd,hqkd->hqk", q_c, k_sel).astype(jnp.float32) * scale
                 + table_h[h_ix, rel_bucket(d_sel)])
        ok_sel = jnp.broadcast_to((idx < own)[..., None],
                                  (H, MOBA_QCHUNK, n_top, MOBA_BLK)).reshape(H, MOBA_QCHUNK, n_keys)
        p = masked_softmax(jnp.concatenate([s_own, s_sel], axis=-1),
                           jnp.concatenate([ok_own, ok_sel], axis=-1)).astype(v.dtype)
        return (jnp.einsum("hqk,khd->qhd", p[..., :MOBA_BLK], v_own)
                + jnp.einsum("hqk,hqkd->qhd", p[..., MOBA_BLK:], v_sel))

    out = lax.map(chunk, jnp.arange(B * n_q))
    return out.reshape(B, S, H * dh) @ w_out

def first_inputs(seed: int = 0) -> dict:
    key = jax.random.key(seed)
    ks = jax.random.split(key, 16)
    f32 = jnp.float32
    hd = N_HEADS * HEAD_DIM

    def nrm(k, shape, fan_in):
        return jax.random.normal(k, shape, f32) * fan_in ** -0.5

    return {
        "x": jax.random.normal(ks[0], (BATCH, SEQ, D_MODEL), f32),
        "rel_bias": 0.5 * jax.random.normal(ks[1], (REL_BUCKETS, N_HEADS), f32),
        "norm_g": 1.0 + 0.05 * jax.random.normal(ks[2], (DEPTH, 6, D_MODEL), f32),
        "ffn_w_in": nrm(ks[3], (DEPTH, 2, D_MODEL, 2 * D_FF), D_MODEL),
        "ffn_w_out": nrm(ks[4], (DEPTH, 2, D_FF, D_MODEL), D_FF),
        "a_w_in": nrm(ks[5], (N_A_LAYERS, D_MODEL, A_IN), D_MODEL),
        "a_w_out": nrm(ks[6], (N_A_LAYERS, hd, D_MODEL), hd),
        "a_sinks": jax.random.normal(ks[7], (N_A_LAYERS, N_HEADS), f32),
        "b_w_in": nrm(ks[8], (N_B_LAYERS, D_MODEL, B_IN), D_MODEL),
        "b_w_out": nrm(ks[9], (N_B_LAYERS, hd, D_MODEL), hd),
        "b_cmp_pos": 0.5 * jax.random.normal(ks[10], (N_B_LAYERS, 2, CMP_LEN, HEAD_DIM), f32),
        "b_cmp_w1": nrm(ks[11], (N_B_LAYERS, 2, CMP_LEN * HEAD_DIM, CMP_HIDDEN), CMP_LEN * HEAD_DIM),
        "b_cmp_w2": nrm(ks[12], (N_B_LAYERS, 2, CMP_HIDDEN, HEAD_DIM), CMP_HIDDEN),
        "c_w_in": nrm(ks[13], (N_C_LAYERS, D_MODEL, C_IN), D_MODEL),
        "c_w_out": nrm(ks[14], (N_C_LAYERS, hd, D_MODEL), hd),
    }

def first_block(x, rel_bias, norm_g, ffn_w_in, ffn_w_out, a_w_in, a_w_out, a_sinks,
              b_w_in, b_w_out, b_cmp_pos, b_cmp_w1, b_cmp_w2, c_w_in, c_w_out):
    for i in range(DEPTH):
        g = norm_g[i]
        x = x + 0.5 * rms_norm(swiglu(rms_norm(x, g[0]), ffn_w_in[i, 0], ffn_w_out[i, 0]), g[1])
        hm = rms_norm(x, g[2])
        kind, j = i % N_MIXERS, i // N_MIXERS
        if kind == 0:
            m = sliding_sink_attention(hm, a_w_in[j], a_w_out[j], a_sinks[j], rel_bias)
        elif kind == 1:
            m = nsa_attention(hm, b_w_in[j], b_w_out[j], b_cmp_pos[j], b_cmp_w1[j],
                              b_cmp_w2[j], rel_bias)
        else:
            m = moba_attention(hm, c_w_in[j], c_w_out[j], rel_bias)
        x = x + rms_norm(m, g[3])
        x = x + 0.5 * rms_norm(swiglu(rms_norm(x, g[4]), ffn_w_in[i, 1], ffn_w_out[i, 1]), g[5])
    return x


DEPTH_2 = 1

GRID_W = 64
N_Q_HEADS = 8
N_KV_HEADS = 2
GQA_GROUP = N_Q_HEADS // N_KV_HEADS
ATTN_W = N_Q_HEADS * HEAD_DIM
KV_W = N_KV_HEADS * HEAD_DIM
Q_BLOCK = 128
ROPE_THETA = 10000.0
SSD_HEAD_DIM = 64
SSD_HEADS = 8
SSD_W = SSD_HEADS * SSD_HEAD_DIM
SSD_GROUPS = 2
HEADS_PER_GROUP = SSD_HEADS // SSD_GROUPS
D_STATE = 64
D_CONV = 7
CONV_CH = SSD_W + 2 * SSD_GROUPS * D_STATE
CHUNK = 128
SPLIT_SIZES = (ATTN_W, KV_W, KV_W, SSD_W, CONV_CH, 2 * SSD_HEADS, 2 * D_MODEL)
IN_PROJ = sum(SPLIT_SIZES)
N_EXPERT_GROUPS = 4
EXPERTS_PER_GROUP = 4
N_EXPERTS = N_EXPERT_GROUPS * EXPERTS_PER_GROUP
TOP_K_IN_GROUP = 2
D_EXPERT = 512
EPS = 1e-6


def rmsnorm(x, w):
    xf = x.astype(jnp.float32)
    xf = xf * lax.rsqrt(jnp.mean(xf * xf, axis=-1, keepdims=True) + EPS)
    return xf.astype(x.dtype) * w

def rotate_half(u):
    u1, u2 = jnp.split(u, 2, axis=-1)
    return jnp.concatenate([-u2, u1], axis=-1)

def axial_rope_tables(seq_len, dtype):
    rows = seq_len // GRID_W
    row = jnp.repeat(jnp.arange(rows, dtype=jnp.int32), GRID_W)
    col = jnp.tile(jnp.arange(GRID_W, dtype=jnp.int32), rows)
    half = HEAD_DIM // 2
    inv_freq = ROPE_THETA ** (-jnp.arange(0, half, 2, dtype=jnp.float32) / half)
    ang_r = row.astype(jnp.float32)[:, None] * inv_freq[None, :]
    ang_c = col.astype(jnp.float32)[:, None] * inv_freq[None, :]
    cos = jnp.concatenate([jnp.cos(ang_r), jnp.cos(ang_r), jnp.cos(ang_c), jnp.cos(ang_c)], axis=-1)
    sin = jnp.concatenate([jnp.sin(ang_r), jnp.sin(ang_r), jnp.sin(ang_c), jnp.sin(ang_c)], axis=-1)
    return cos.astype(dtype), sin.astype(dtype)

def apply_axial_rope(x, cos, sin):
    xr, xc = jnp.split(x, 2, axis=-1)
    rot = jnp.concatenate([rotate_half(xr), rotate_half(xc)], axis=-1)
    return x * cos[None, :, None, :] + rot * sin[None, :, None, :]

def gqa_attention(q, k, v, q_norm_w, k_norm_w, cos, sin):
    b, s = q.shape[0], q.shape[1]
    q = apply_axial_rope(rmsnorm(q, q_norm_w), cos, sin)
    k = apply_axial_rope(rmsnorm(k, k_norm_w), cos, sin)
    scale = 1.0 / math.sqrt(HEAD_DIM)
    nb = s // Q_BLOCK
    qb = jnp.moveaxis(q.reshape(b, nb, Q_BLOCK, N_KV_HEADS, GQA_GROUP, HEAD_DIM), 1, 0)

    def one_block(qblk):
        scores = jnp.einsum('bqkgd,bskd->bkgqs', qblk, k).astype(jnp.float32) * scale
        p = jax.nn.softmax(scores, axis=-1).astype(v.dtype)
        return jnp.einsum('bkgqs,bskd->bqkgd', p, v)

    o = lax.map(one_block, qb)
    return jnp.moveaxis(o, 0, 1).reshape(b, s, ATTN_W)

def depthwise_centred_conv(u, w, bias):
    pad = (D_CONV - 1) // 2
    y = lax.conv_general_dilated(u, w[:, None, :], window_strides=(1,), padding=[(pad, pad)],
                                 dimension_numbers=('NWC', 'WIO', 'NWC'),
                                 feature_group_count=u.shape[-1])
    return y + bias

def ssd_chunked(x, dt, a, bm, cm):
    b, L, h, p = x.shape
    n = bm.shape[-1]
    c = L // CHUNK
    xc = x.reshape(b, c, CHUNK, h, p)
    dtc = dt.reshape(b, c, CHUNK, h)
    bc = bm.reshape(b, c, CHUNK, h, n)
    cc = cm.reshape(b, c, CHUNK, h, n)
    a_cum = jnp.cumsum(dtc * a, axis=2)
    seg = a_cum[:, :, :, None, :] - a_cum[:, :, None, :, :]
    tril = jnp.tril(jnp.ones((CHUNK, CHUNK), dtype=bool))[None, None, :, :, None]
    decay = jnp.exp(jnp.where(tril, seg, -jnp.inf))
    xdt = xc * dtc[..., None]
    cb = jnp.einsum('bcihn,bcjhn->bcijh', cc, bc)
    y_diag = jnp.einsum('bcijh,bcjhp->bcihp', cb * decay, xdt)
    decay_to_end = jnp.exp(a_cum[:, :, -1:, :] - a_cum)
    states = jnp.einsum('bcjhn,bcjhp->bchpn', bc * decay_to_end[..., None], xdt)
    chunk_decay = jnp.exp(a_cum[:, :, -1, :])

    def step(carry, inp):
        s_c, d_c = inp
        return carry * d_c[:, :, None, None] + s_c, carry

    h0 = jnp.zeros((b, h, p, n), dtype=x.dtype)
    _, states_in = lax.scan(step, h0, (jnp.moveaxis(states, 1, 0), jnp.moveaxis(chunk_decay, 1, 0)))
    states_in = jnp.moveaxis(states_in, 0, 1)
    y_off = jnp.einsum('bcihn,bchpn->bcihp', cc, states_in) * jnp.exp(a_cum)[..., None]
    return (y_diag + y_off).reshape(b, L, h, p)

def bidirectional_ssd(z, xbc, dt_raw, conv_w, conv_b, dt_bias, a_log, d_skip, norm_w):
    b, s = xbc.shape[0], xbc.shape[1]
    xbc = jax.nn.silu(depthwise_centred_conv(xbc, conv_w, conv_b))
    xs, bm, cm = jnp.split(xbc, [SSD_W, SSD_W + SSD_GROUPS * D_STATE], axis=-1)
    f32 = jnp.float32
    xs = xs.reshape(b, s, SSD_HEADS, SSD_HEAD_DIM).astype(f32)
    bm = jnp.repeat(bm.reshape(b, s, SSD_GROUPS, D_STATE), HEADS_PER_GROUP, axis=2).astype(f32)
    cm = jnp.repeat(cm.reshape(b, s, SSD_GROUPS, D_STATE), HEADS_PER_GROUP, axis=2).astype(f32)
    dt = jax.nn.softplus(dt_raw.reshape(b, s, 2, SSD_HEADS).astype(f32) + dt_bias.astype(f32))
    a = -jnp.exp(a_log.astype(f32))
    y_fwd = ssd_chunked(xs, dt[:, :, 0], a[0], bm, cm)
    flip = lambda u: jnp.flip(u, axis=1)
    y_bwd = flip(ssd_chunked(flip(xs), flip(dt[:, :, 1]), a[1], flip(bm), flip(cm)))
    y = y_fwd + y_bwd + d_skip.astype(f32)[None, None, :, None] * xs
    y = y.reshape(b, s, SSD_W).astype(z.dtype)
    return rmsnorm(y * jax.nn.silu(z), norm_w)

def hierarchical_moe(h, w_rg, b_rg, w_re, b_re, w1, w3, w2):
    b, s, d = h.shape
    t = h.reshape(b * s, d)
    p_group = jax.nn.softmax((t @ w_rg + b_rg).astype(jnp.float32), axis=-1)
    g_val, g_idx = lax.top_k(p_group, 1)
    fine = (t @ w_re + b_re).astype(jnp.float32).reshape(-1, N_EXPERT_GROUPS, EXPERTS_PER_GROUP)
    fine_sel = jnp.take_along_axis(fine, g_idx[:, :, None], axis=1)[:, 0]
    e_val, e_idx = lax.top_k(jax.nn.softmax(fine_sel, axis=-1), TOP_K_IN_GROUP)
    e_val = e_val / jnp.sum(e_val, axis=-1, keepdims=True)
    within = jnp.sum(jax.nn.one_hot(e_idx, EXPERTS_PER_GROUP, dtype=jnp.float32) * e_val[..., None], axis=1)
    combine = (jax.nn.one_hot(g_idx[:, 0], N_EXPERT_GROUPS, dtype=jnp.float32)[:, :, None]
               * within[:, None, :] * g_val[:, :, None]).reshape(-1, N_EXPERTS).astype(t.dtype)
    out = jnp.zeros_like(t)
    for e in range(N_EXPERTS):
        y_e = (jax.nn.silu(t @ w1[e]) * (t @ w3[e])) @ w2[e]
        out = out + combine[:, e:e + 1] * y_e
    return out.reshape(b, s, d)

def second_inputs(seed: int = 0) -> dict:
    key = jax.random.key(seed)
    ks = jax.random.split(key, 24)
    f32 = jnp.float32
    L = DEPTH_2

    def nrm(k, shape, fan_in):
        return jax.random.normal(k, shape, f32) * (fan_in ** -0.5)

    def gain(k, shape):
        return 1.0 + 0.02 * jax.random.normal(k, shape, f32)

    dt0 = jnp.exp(jax.random.uniform(ks[9], (L, 2, SSD_HEADS), f32, math.log(1e-3), math.log(1e-1)))
    dt_bias = dt0 + jnp.log(-jnp.expm1(-dt0))
    return {
        "x": jax.random.normal(ks[0], (BATCH, SEQ, D_MODEL), f32),
        "norm_mix_w": gain(ks[1], (L, D_MODEL)),
        "w_in": nrm(ks[2], (L, D_MODEL, IN_PROJ), D_MODEL),
        "b_gate": 0.02 * jax.random.normal(ks[3], (L, 2 * D_MODEL), f32),
        "q_norm_w": gain(ks[4], (L, HEAD_DIM)),
        "k_norm_w": gain(ks[5], (L, HEAD_DIM)),
        "w_attn_o": nrm(ks[6], (L, ATTN_W, D_MODEL), ATTN_W),
        "conv_w": nrm(ks[7], (L, D_CONV, CONV_CH), D_CONV),
        "conv_b": 0.02 * jax.random.normal(ks[8], (L, CONV_CH), f32),
        "dt_bias": dt_bias,
        "a_log": jnp.log(jax.random.uniform(ks[10], (L, 2, SSD_HEADS), f32, 1.0, 16.0)),
        "d_skip": 1.0 + 0.1 * jax.random.normal(ks[11], (L, SSD_HEADS), f32),
        "ssd_norm_w": gain(ks[12], (L, SSD_W)),
        "w_ssd_o": nrm(ks[13], (L, SSD_W, D_MODEL), SSD_W),
        "w_out": nrm(ks[14], (L, D_MODEL, D_MODEL), D_MODEL),
        "norm_ffn_w": gain(ks[15], (L, D_MODEL)),
        "w_router_group": nrm(ks[16], (L, D_MODEL, N_EXPERT_GROUPS), D_MODEL),
        "b_router_group": 0.01 * jax.random.normal(ks[17], (L, N_EXPERT_GROUPS), f32),
        "w_router_expert": nrm(ks[18], (L, D_MODEL, N_EXPERTS), D_MODEL),
        "b_router_expert": 0.01 * jax.random.normal(ks[19], (L, N_EXPERTS), f32),
        "w1": nrm(ks[20], (L, N_EXPERTS, D_MODEL, D_EXPERT), D_MODEL),
        "w3": nrm(ks[21], (L, N_EXPERTS, D_MODEL, D_EXPERT), D_MODEL),
        "w2": nrm(ks[22], (L, N_EXPERTS, D_EXPERT, D_MODEL), D_EXPERT),
    }

def second_block(x, norm_mix_w, w_in, b_gate, q_norm_w, k_norm_w, w_attn_o, conv_w, conv_b,
              dt_bias, a_log, d_skip, ssd_norm_w, w_ssd_o, w_out, norm_ffn_w,
              w_router_group, b_router_group, w_router_expert, b_router_expert, w1, w3, w2):
    b, s, _ = x.shape
    cos, sin = axial_rope_tables(s, x.dtype)
    split_at = [int(v) for v in np.cumsum(SPLIT_SIZES)[:-1]]
    for l in range(DEPTH_2):
        h = rmsnorm(x, norm_mix_w[l])
        proj = h @ w_in[l]
        q, k, v, z, xbc, dt_raw, gates = jnp.split(proj, split_at, axis=-1)
        q = q.reshape(b, s, N_Q_HEADS, HEAD_DIM)
        k = k.reshape(b, s, N_KV_HEADS, HEAD_DIM)
        v = v.reshape(b, s, N_KV_HEADS, HEAD_DIM)
        attn = gqa_attention(q, k, v, q_norm_w[l], k_norm_w[l], cos, sin)
        ssd = bidirectional_ssd(z, xbc, dt_raw, conv_w[l], conv_b[l], dt_bias[l],
                                a_log[l], d_skip[l], ssd_norm_w[l])
        g_attn, g_ssd = jnp.split(jax.nn.sigmoid(gates + b_gate[l]), 2, axis=-1)
        merged = g_attn * (attn @ w_attn_o[l]) + g_ssd * (ssd @ w_ssd_o[l])
        x = x + merged @ w_out[l]
        h2 = rmsnorm(x, norm_ffn_w[l])
        x = x + hierarchical_moe(h2, w_router_group[l], b_router_group[l], w_router_expert[l],
                                 b_router_expert[l], w1[l], w3[l], w2[l])
    return x


def setup_inputs(seed=0):
    out = dict(first_inputs(seed))
    for name, value in second_inputs(seed + 1).items():
        if name != "x":
            out[name + "_2"] = value
    return out


def reference(
    x, rel_bias, norm_g, ffn_w_in, ffn_w_out, a_w_in, a_w_out, a_sinks, b_w_in, b_w_out,
    b_cmp_pos, b_cmp_w1, b_cmp_w2, c_w_in, c_w_out, norm_mix_w_2, w_in_2, b_gate_2, q_norm_w_2,
    k_norm_w_2, w_attn_o_2, conv_w_2, conv_b_2, dt_bias_2, a_log_2, d_skip_2, ssd_norm_w_2,
    w_ssd_o_2, w_out_2, norm_ffn_w_2, w_router_group_2, b_router_group_2, w_router_expert_2,
    b_router_expert_2, w1_2, w3_2, w2_2,
):
    x = first_block(
        x, rel_bias, norm_g, ffn_w_in, ffn_w_out, a_w_in, a_w_out, a_sinks, b_w_in, b_w_out,
        b_cmp_pos, b_cmp_w1, b_cmp_w2, c_w_in, c_w_out,
    )
    return second_block(
        x, norm_mix_w_2, w_in_2, b_gate_2, q_norm_w_2, k_norm_w_2, w_attn_o_2, conv_w_2,
        conv_b_2, dt_bias_2, a_log_2, d_skip_2, ssd_norm_w_2, w_ssd_o_2, w_out_2, norm_ffn_w_2,
        w_router_group_2, b_router_group_2, w_router_expert_2, b_router_expert_2, w1_2, w3_2,
        w2_2,
    )


_drawn_inputs = setup_inputs


def setup_inputs(seed=0):
    import zlib

    import numpy as np

    out = dict(_drawn_inputs(seed))
    spreads = {}
    factors = {'norm_mix_w_2': 8.0,
     'b_gate_2': 8.0,
     'q_norm_w_2': 8.0,
     'k_norm_w_2': 8.0,
     'conv_b_2': 8.0,
     'dt_bias_2': 3.019,
     'd_skip_2': 81.421,
     'ssd_norm_w_2': 8.0,
     'norm_ffn_w_2': 7.272,
     'b_router_group_2': 8.0,
     'b_router_expert_2': 33.271}
    for name, (base, spread) in spreads.items():
        noise = np.random.default_rng([zlib.crc32(name.encode()), seed]).standard_normal(out[name].shape)
        drawn = base * np.exp(spread * noise) if base else spread * noise
        out[name] = __import__('jax').numpy.asarray(drawn.astype(out[name].dtype))
    for name, factor in factors.items():
        out[name] = (out[name] * factor).astype(out[name].dtype)
    return out
```

```python
from contextlib import ExitStack

import numpy as np

import concourse.bass as bass
from concourse import mybir

F32 = mybir.dt.float32
F32R = mybir.dt.float32r
I32 = mybir.dt.int32
ALU = mybir.AluOpType
ACT = mybir.ActivationFunctionType
AX = mybir.AxisListType.X

P = 128
SEQ = 256
NT = SEQ // P
D = 1024
KT = D // P
HD = 64
NH = 16
DFF = 2816
PAIR = 256
NPAIR = DFF // PAIR
NEXP = 16
DEXP = 512
EPS = 1e-6
NEG = -1e30
TINY = 1e-30
SCALE = HD ** -0.5
RING = 3
SLOT = 3 * KT * PAIR
RSQRT_MAGIC = 0x5F3759DF

N_CMP = 15
CMP_STRIDE = 16
CMP_LEN = 32
CMP_ROW_TILES = CMP_LEN * HD // P
G_B = 4
DTOEP = 384

C_ID = 0
C_CMPM = C_ID + P
C_CMPOK = C_CMPM + NT * N_CMP
C_ONE = C_CMPOK + NT * N_CMP
C_MHALF = C_ONE + 1
C_REV = C_MHALF + 1
C_TOEPM = C_REV + P
C_HOT = C_TOEPM + 2 * DTOEP
C_FIRST = C_HOT + DTOEP
C_COS = C_FIRST
C_SIN = C_COS + NT * HD
C_TRI = C_SIN + NT * HD
C_IDX = C_TRI + 2 * NT * SEQ
C_ONES = C_IDX + 4
C_END = C_ONES + P

H_Q = 8 * HD
H_QK = H_Q + 2 * HD
SSD_H = 8
SSD_W = SSD_H * HD
CONV_K = 7
CONV_T = 6
CONV_PAD = (CONV_K - 1) // 2


def bucket_of(dist):
    dist = np.maximum(dist, 0)
    d = np.maximum(dist, 1).astype(np.float32)
    log_b = 16 + (np.log(d / np.float32(16)) / np.float32(np.log(64.0)) * np.float32(16)).astype(np.int32)
    return np.where(dist < 16, dist, np.minimum(log_b, 31))


def make_consts():
    c = np.zeros((P, C_END), np.float32)
    c[:, C_ID:C_ID + P] = np.eye(P)
    t = np.arange(SEQ).reshape(NT, P)
    ok = (np.arange(N_CMP) * CMP_STRIDE + CMP_LEN - 1)[None, None, :] <= t[:, :, None]
    c[:, C_CMPM:C_CMPM + NT * N_CMP] = np.where(ok, 0.0, NEG).transpose(1, 0, 2).reshape(P, -1)
    c[:, C_CMPOK:C_CMPOK + NT * N_CMP] = ok.transpose(1, 0, 2).reshape(P, -1)
    c[:, C_ONE] = 1.0
    c[:, C_MHALF] = -0.5
    c[:, C_REV:C_REV + P] = np.eye(P)[::-1]
    dist = SEQ - 1 - np.arange(DTOEP)
    c[:NH, C_TOEPM:C_TOEPM + DTOEP] = np.where(dist < 0, NEG, 0.0)
    c[:NH, C_TOEPM + DTOEP:C_TOEPM + 2 * DTOEP] = np.where((dist < 0) | (dist >= 128), NEG, 0.0)
    c[:32, C_HOT:C_HOT + DTOEP] = np.arange(32)[:, None] == bucket_of(dist)[None, :]
    pos = np.arange(SEQ)
    inv = 10000.0 ** (-np.arange(0, 32, 2, dtype=np.float32) / 32)
    inv = inv.astype(np.float32)
    ang_r = (pos // 64).astype(np.float32)[:, None] * inv[None, :]
    ang_c = (pos % 64).astype(np.float32)[:, None] * inv[None, :]
    cos = np.concatenate([np.cos(ang_r), np.cos(ang_r), np.cos(ang_c), np.cos(ang_c)], 1)
    sin = np.concatenate([-np.sin(ang_r), np.sin(ang_r), -np.sin(ang_c), np.sin(ang_c)], 1)
    c[:, C_COS:C_COS + NT * HD] = cos.reshape(NT, P, HD).transpose(1, 0, 2).reshape(P, -1)
    c[:, C_SIN:C_SIN + NT * HD] = sin.reshape(NT, P, HD).transpose(1, 0, 2).reshape(P, -1)
    j, i = np.arange(SEQ)[:, None], np.arange(SEQ)[None, :]
    tri = np.stack([j <= i, j >= i]).astype(np.float32).reshape(2, NT, P, SEQ)
    c[:, C_TRI:C_TRI + 2 * NT * SEQ] = tri.transpose(2, 0, 1, 3).reshape(P, -1)
    c[:, C_IDX:C_IDX + 4] = [4, 3, 2, 1]
    c[:, C_ONES:C_ONES + P] = 1.0
    return c


def block_list(which=None):
    blocks = []
    for i in range(4):
        blocks.append(dict(kind="ffn", layer=i, sub=0))
        blocks.append(dict(kind="ABCA"[i], layer=i, j=i // 3))
        blocks.append(dict(kind="ffn", layer=i, sub=1))
    blocks.append(dict(kind="H"))
    blocks.append(dict(kind="moe"))
    return blocks if which is None else [blocks[i] for i in which]


class Attn:

    def __init__(self, kind):
        self.kind = kind
        self.tiles = 4 if kind == "H" else 8
        self.gqa = kind != "C"
        self.quads = list(range(self.tiles // 2))

    def ktile(self, quad, t, s):
        return {"A": quad // 2, "B": quad + 4 * s, "C": 2 * quad + t, "H": quad}[self.kind]

    def vcol(self, quad, r, s):
        return {"A": quad // 2, "B": quad + 4 * s, "C": 4 * quad + r, "H": quad}[self.kind] * HD


class Semaphores:

    def __init__(self, nc, ctx):
        def some(names):
            return [ctx.enter_context(nc.semaphore(n)) for n in names.split()]

        self.raw0, self.raw1, self.raw2, self.slots_used = \
            some("raw0 raw1 raw2 slots_used")
        self.gain0, self.gain1, self.x_in, self.consts_in = \
            some("gain0 gain1 x_in consts_in")
        self.bias_rows_in, self.bias_tab, self.bias_ps, self.bias_sum, self.bias_rows_out, self.bias_in = \
            some("bias_rows_in bias_tab bias_ps bias_sum bias_rows_out bias_in")
        self.bias_product, self.bias_turned, self.sinks_in = \
            some("bias_product bias_turned sinks_in")
        self.mean_sq, self.power = some("mean_sq power")
        self.ss_done, self.xs_ready, self.tr_done, self.hT_act, self.hT_dve, self.y_done = \
            some("ss_done xs_ready tr_done hT_act hT_dve y_done")
        self.post_used, = some("post_used")
        self.gu_hi, self.dn_hi, self.gu_lo, self.dn_lo, self.gu_done, self.silu = \
            some("gu_hi dn_hi gu_lo dn_lo gu_done silu")
        self.sgc, self.hid_done, self.hid_hi, self.hid_lo, self.down_done = \
            some("sgc hid_done hid_hi hid_lo down_done")
        self.proj, self.evac_act, self.evac_dve = \
            some("proj evac_act evac_dve")
        self.scores, self.sbias, self.smax, self.sexp, self.coef, self.psc = \
            some("scores sbias smax sexp coef psc")
        self.pT, self.pT_sb, self.oPV, self.oT_sb = \
            some("pT pT_sb oPV oT_sb")
        self.bgate, self.cmp_small, self.z2, self.chid_ps, self.gelu, self.chidT_ps = \
            some("bgate cmp_small z2 chid_ps gelu chidT_ps")
        self.chidT, self.kcb_ps, self.kcb, self.s_cmp, self.cmp_arg, self.cmp_exp = \
            some("chidT kcb_ps kcb s_cmp cmp_arg cmp_exp")
        self.pc, = some("pc")
        self.h_rows, self.h_small, self.h_sq, self.h_rope, self.h_qk_ps, self.h_qT = \
            some("h_rows h_small h_sq h_rope h_qk_ps h_qT")
        self.h_kT, self.h_ao, self.h_merge1, self.h_conv, self.h_silu, self.h_dtarg = \
            some("h_kT h_ao h_merge1 h_conv h_silu h_dtarg")
        self.h_dtexp, self.h_dta, self.h_acol_ps, self.h_cb_ps, self.h_xt_ps, self.h_row = \
            some("h_dtexp h_dta h_acol_ps h_cb_ps h_xt_ps h_row")
        self.h_arg, self.h_exp, self.h_y, self.h_yss, self.h_yn, self.h_yT_ps = \
            some("h_arg h_exp h_y h_yss h_yn h_yT_ps")
        self.h_yT, self.h_so, self.h_merge2, self.h_mT_ps, self.h_mT, self.h_zs = \
            some("h_yT h_so h_merge2 h_mT_ps h_mT h_zs")
        self.h_w_sum, = some("h_w_sum")
        self.e_small, self.e_hT, self.e_lg, self.e_arg, self.e_exp, self.e_comb = \
            some("e_small e_hT e_lg e_arg e_exp e_comb")
        self.e_rows, self.e_act, self.comb = \
            some("e_rows e_act comb")
        self.chain_act, self.chain_dve, self.out_done = \
            some("chain_act chain_dve out_done")


class Program:

    def __init__(self, nc, ins, out, blocks, ctx):
        self.nc, self.ins, self.out, self.blocks = nc, ins, out, blocks
        self.ctx = ctx
        self.map_memory()
        self.name_semaphores()
        self.plan()

    def map_memory(self):
        nc = self.nc
        self.top = 16640

        def at(name, shape, off, dt=F32):
            return nc.alloc_sbuf_tensor_at(name, shape, dt, offset=off)

        def new(name, shape, dt=F32):
            n = 4
            for s in shape[1:]:
                n *= s
            t = at(name, shape, self.top, dt)
            self.top += (n + 31) // 32 * 32
            return t

        self.at = at
        self.x = new("x_res", [P, NT, D])
        self.xs = new("x_scaled", [P, NT, D])
        self.hT = new("hT", [P, KT, SEQ])
        self.gain = [new(f"gain{i}", [P, D]) for i in range(2)]
        self.raw = new("raw_ring", [P, RING, SLOT])
        self.arena = self.top
        self.hT_hi = new("hT_hi", [P, KT, SEQ], F32R)
        self.hT_lo = new("hT_lo", [P, KT, SEQ], F32R)
        self.gu_hi = new("gu_hi", [P, 2, 2 * KT, P], F32R)
        self.gu_lo = new("gu_lo", [P, 2, 2 * KT, P], F32R)
        self.dn_hi = new("down_hi", [P, 2, D], F32R)
        self.dn_lo = new("down_lo", [P, 2, D], F32R)
        self.sg = new("silu_gate", [P, 2, SEQ])
        self.hid = new("hidden", [P, 2, SEQ])
        self.hid_hi = new("hidden_hi", [P, 2, SEQ], F32R)
        self.hid_lo = new("hidden_lo", [P, 2, SEQ], F32R)
        self.arena_end = self.top
        self.cur = self.arena

        def mix(name, shape):
            n = 4
            for s in shape[1:]:
                n *= s
            t = at(name, shape, self.cur)
            self.cur += (n + 31) // 32 * 32
            assert self.cur <= self.arena_end, name
            return t

        self.oT = mix("oT", [P, 8, SEQ])
        self.kT = mix("kT", [P, 8, SEQ])
        self.v = mix("v_tok", [P, NT, D])
        self.qT = mix("qT", [P, 8, SEQ])
        self.S = mix("scores", [P, 2, 4, SEQ])
        self.PT = mix("probsT", [P, 2, NT, 4 * P])
        b_start = self.cur
        self.zc = mix("cmp_tokens", [P, 2, G_B, SEQ])
        self.z2 = mix("cmp_blocks", [P, 2, CMP_ROW_TILES, G_B * N_CMP])
        self.chid = mix("cmp_hidden", [P, 2, SEQ])
        self.chidT = mix("cmp_hiddenT", [P, 2, 2, G_B * N_CMP])
        self.kcb = mix("cmp_keysT", [P, G_B * N_CMP])
        self.vcb = mix("cmp_values", [P, G_B, HD])
        self.cw2 = mix("cmp_w2", [P, 2, 2, HD])
        self.cpos = mix("cmp_pos", [P, 2, CMP_ROW_TILES])
        self.pc = mix("cmp_probs", [P, NT, NH, N_CMP])
        self.bgate = mix("b_gate", [P, NT, 48])
        h_start = b_start
        self.bias = new("bias_full", [P, NH, SEQ])
        self.biasA = new("bias_window", [P, NH, P])
        self.rows_hot = at("rows_hot", [32, DTOEP], self.arena)[:, :]
        self.rows_mask = at("rows_mask", [NH, 2, DTOEP], self.arena + 4 * DTOEP)[:, :, :]
        self.rows_tab = at("rows_tab", [32, NH], self.arena + 12 * DTOEP)[:, :]
        self.rows_raw = at("rows_raw", [32, NH], self.arena + 32 * DTOEP)[:, :]
        self.rows_sum = at("rows_sum", [NH, 2, DTOEP], self.arena + 12 * DTOEP + 64)[:, :, :]
        bias_end = self.top
        self.z = at("h_z", [P, NT, SSD_W], self.arena + 4 * 4 * SEQ)
        self.xT = at("h_xbcT", [P, CONV_T, SEQ], self.arena + 4 * 10 * SEQ)
        self.ssdT = at("h_ssdT", [P, 4, SEQ], self.arena + 8 * 4 * SEQ * 2 + 4 * NT * D + 4 * 4 * SEQ)
        self.cur = h_start

        def hyb(name, shape, limit=bias_end):
            n = 4
            for k in shape[1:]:
                n *= k
            t = at(name, shape, self.cur)
            self.cur += (n + 31) // 32 * 32
            assert self.cur <= limit, (name, self.cur, limit)
            return t

        self.gates = hyb("h_gates", [P, NT, 2 * D])
        self.xbc = hyb("h_xbc", [P, CONV_T, SEQ + 2 * CONV_PAD])
        self.cb = at("h_cb", [P, 2, NT, SEQ], self.cur - 4 * CONV_T * (SEQ + 2 * CONV_PAD) // 32 * 32)
        self.xtok = hyb("h_xtok", [P, NT, SSD_W])
        self.qk = hyb("h_qk", [P, NT, H_QK])
        self.ysd = hyb("h_y", [P, NT, SSD_W])
        self.c2 = hyb("h_consts", [P, C_END - C_FIRST])
        self.cw = hyb("h_conv_w", [P, CONV_T, CONV_K])
        self.cbias = hyb("h_conv_b", [P, CONV_T])
        self.dtb = hyb("h_dt_bias", [P, 2 * SSD_H])
        self.alog = hyb("h_a_log", [P, 2 * SSD_H])
        self.dskip = hyb("h_d_skip", [P, SSD_H])
        self.qkw = hyb("h_qk_norm", [P, 2, HD])
        self.ssdw = hyb("h_ssd_norm", [P, SSD_W])
        self.dt = hyb("h_dt", [P, NT, 2 * SSD_H])
        self.dta = hyb("h_dta", [P, NT, 2 * SSD_H])
        self.acol = hyb("h_acum", [P, NT, 2 * SSD_H])
        self.dts = hyb("h_dt_scratch", [P, 5, NT * 2 * SSD_H])
        self.qkr = hyb("h_qk_stats", [P, 2, NT * 10])
        self.bgrow = self.at("h_gate_bias", [1, 2 * D], self.arena + 4 * (4 * 8 * SEQ))
        o = self.arena + 4 * (4 * 8 * SEQ)
        self.dec = at("h_decay", [P, 4, SEQ], o)
        self.wgt = at("h_weights", [P, 4, SEQ], o + 4 * 4 * SEQ)
        self.mm = at("h_mix", [P, 2, NT, SEQ], o + 8 * 4 * SEQ)
        self.cur = self.arena_end
        self.comb_bc = hyb("e_weights_all", [P, NEXP, SEQ])
        self.rw = hyb("e_router_w", [P, KT, 20])
        self.rb = hyb("e_router_b", [1, 20])
        self.lg = hyb("e_logits", [P, NT, 20])
        self.r4 = hyb("e_four", [P, 12, NT, 4])
        self.r1 = hyb("e_one", [P, 12, NT])
        self.p16 = hyb("e_sixteen", [P, NT, NEXP])
        self.comb = hyb("e_weights", [P, NT, NEXP])
        self.eidx = hyb("e_consts", [P, 4 + P])
        self.uses_bias = any(b["kind"] in "ABC" for b in self.blocks)

        self.cst = new("consts_sb", [P, C_TOEPM])
        self.sink = new("sinks", [P, 2, NH])
        self.sink_raw = new("sinks_in", [P, 2 * NH])
        self.st = new("stats", [P, 64])
        self.nt = new("newton", [P, 3, 32])
        self.am = new("attn_max", [P, 2, 4])
        self.den = new("attn_den", [P, 2, 4])
        self.se = new("attn_sink_exp", [P, 2, 4])
        self.coef = new("attn_coef", [P, 2, 4])
        self.cs = new("cmp_stats", [P, 4, NH])
        assert self.top <= 229344, self.top
        self.psum = self.ctx.enter_context(nc.psum_tensor("psum_all", [P, 8, 512], F32))
        self.ident = self.cst[:, C_ID:C_ID + P]
        self.one = self.cst[:, C_ONE:C_ONE + 1]
        self.minus_half = self.cst[:, C_MHALF:C_MHALF + 1]
        self.scratch = nc.dram_tensor("bias_rows", (2, NH, DTOEP), F32, kind="Internal").ap()

    def name_semaphores(self):
        self.sem = Semaphores(self.nc, self.ctx)
        self.sem_raw = [self.sem.raw0, self.sem.raw1, self.sem.raw2]
        self.sem_gain = [self.sem.gain0, self.sem.gain1]
        self.chain = {"act": 0, "dve": 0, "pool": 0}

    def plan(self):
        ins = self.ins
        fill = tile = item = unit = sunit = outs = 0
        split = used = 0
        self.fills = []
        for n, b in enumerate(self.blocks):
            b["n"], b["fill0"], b["tile0"], b["item0"], b["unit0"] = n, fill, tile, item, unit
            kind = b["kind"]
            if kind in ("ffn", "moe"):
                b["pairs"] = NPAIR if kind == "ffn" else NEXP * DEXP // PAIR
                b["tiles"] = 2 * b["pairs"]
                for _ in range(b["pairs"]):
                    self.fills.append(("split", split))
                    split += 1
                fill += b["pairs"]
                tile += b["tiles"]
            else:
                b["attn"] = Attn(kind)
                b["loads"], b["items"] = self.mixer_layout(b)
                for f in range(len(b["loads"])):
                    self.fills.append(("used", used))
                    used += 1
                fill += len(b["loads"])
                item += len(b["items"])
                b["units"] = units_of(b)
                b["sunit0"], b["out0"] = sunit, outs
                unit += len(b["units"])
                sunit += sum(u["si"] is not None for u in b["units"])
                outs += NT * len(b["attn"].quads)
        self.gains = []
        for b in self.blocks:
            if b["kind"] == "ffn":
                o = 4 * b["sub"]
                g = ins["norm_g"]
                self.gains += [g[b["layer"], o:o + 1, :], g[b["layer"], o + 1:o + 2, :]]
            elif b["kind"] in "ABC":
                g = ins["norm_g"]
                self.gains += [g[b["layer"], 2:3, :], g[b["layer"], 3:4, :]]
            elif b["kind"] == "H":
                self.gains += [ins["norm_mix_w_2"][0:1, :], ins["norm_mix_w_2"][0:1, :]]
            else:
                self.gains += [ins["norm_ffn_w_2"][0:1, :], ins["norm_ffn_w_2"][0:1, :]]

    def mixer_layout(self, b):
        ins, kind = self.ins, b["kind"]
        loads, items = [], []

        def cols(w, *ranges):
            loads.append(("cols", w, ranges))
            return len(loads) - 1

        def T(f, c0, dst, **kw):
            items.append(dict(form="T", fill=f, c0=c0, dst=dst, **kw))

        def N(f, c0, n, dsts, **kw):
            for a in range(NT):
                items.append(dict(form="N", fill=f, a=a, c0=c0, n=n, dst=dsts[a], **kw))

        def queries(w):
            for c in range(2):
                f = cols(w, (512 * c, 512))
                for r in range(4):
                    T(f, 128 * r, self.qT[:, 4 * c + r, :])

        if kind == "A":
            w = ins["a_w_in"][b["j"]]
            queries(w)
            f = cols(w, (1024, 256))
            T(f, 0, None, both=0)
            N(f, 128, 128, [self.v[:, a, 0:128] for a in range(NT)])
            wo = ins["a_w_out"][b["j"]]
        elif kind == "B":
            w = ins["b_w_in"][0]
            queries(w)
            f = cols(w, (1024, 512))
            for kv in range(2):
                for c in range(2):
                    T(f, 256 * kv + 128 * c, None, zc=(kv, c))
            for s in range(2):
                f = cols(w, (1536 + 512 * s, 512 + 48 * s))
                for c in range(2):
                    T(f, 128 * c, None, both=4 * s + 2 * c)
                N(f, 256, 256, [self.v[:, a, 256 * s:256 * s + 256] for a in range(NT)])
            N(f, 512, 48, [self.bgate[:, a, :] for a in range(NT)])
            b["w1_fill"] = len(loads)
            for kv in range(2):
                loads.append(("rows", ins["b_cmp_w1"][0, kv], 0, CMP_ROW_TILES))
            wo = ins["b_w_out"][0]
        elif kind == "C":
            w = ins["c_w_in"][0]
            for part, dst in ((0, self.qT), (1, self.kT)):
                for c in range(2):
                    f = cols(w, (part * D + 512 * c, 512))
                    for r in range(4):
                        T(f, 128 * r, dst[:, 4 * c + r, :])
            for c in range(2):
                f = cols(w, (2 * D + 512 * c, 512))
                N(f, 0, 512, [self.v[:, a, 512 * c:512 * c + 512] for a in range(NT)])
            wo = ins["c_w_out"][0]
        else:
            w = ins["w_in_2"][0]
            f = cols(w, (0, H_QK))
            N(f, 0, H_Q, [self.qk[:, a, 0:H_Q] for a in range(NT)])
            N(f, H_Q, 128, [self.qk[:, a, H_Q:] for a in range(NT)])
            f = cols(w, (H_QK, 128 + SSD_W))
            N(f, 0, 128, [self.v[:, a, 0:128] for a in range(NT)])
            N(f, 128, SSD_W, [self.z[:, a, :] for a in range(NT)])
            c0 = H_QK + 128 + SSD_W
            for f0, tiles, extra in ((0, 4, 0), (4, 2, 2 * SSD_H)):
                f = cols(w, (c0 + f0 * P, tiles * P + extra))
                for t in range(tiles):
                    T(f, t * P, self.xbc[:, f0 + t, CONV_PAD:CONV_PAD + SEQ])
            N(f, 2 * P, 2 * SSD_H, [self.dt[:, a, :] for a in range(NT)])
            c0 += CONV_T * P + 2 * SSD_H
            for g in range(4):
                f = cols(w, (c0 + 512 * g, 512))
                N(f, 0, 512, [self.gates[:, a, 512 * g:512 * g + 512] for a in range(NT)], row=512 * g)
            b["ao_fill"] = len(loads)
            loads.append(("rows", ins["w_attn_o_2"][0], 0, 4))
            b["so_fill"] = len(loads)
            loads.append(("rows", ins["w_ssd_o_2"][0], 0, 4))
            wo = ins["w_out_2"][0]
        b["wo_fill"] = len(loads)
        for c in range(2):
            loads.append(("rows", wo, 4 * c, 4))
        return loads, items

    def link(self, engine, name, ins):
        self.chain[name] += 1
        sem = self.sem.chain_dve if name == "dve" else self.sem.chain_act
        ins.then_inc(sem, 1)
        engine.wait_ge(sem, self.chain[name])

    def fill_of(self, b, f):
        n = b["fill0"] + f
        return n % RING, 16 * (n + 1)


def stream_weights(K, sp):
    ins = K.ins

    def wait_free(n):
        if n >= RING:
            how, k = K.fills[n - RING]
            if how == "split":
                sp.wait_ge(K.sem.dn_lo, 2 * (k + 1))
            else:
                sp.wait_ge(K.sem.slots_used, k + 1)

    def wait_landed(j, n):
        if n >= 1:
            sp.wait_ge(K.sem_raw[j], 16 * n)

    def slot_view(slot):
        return K.raw[:, slot, :]

    def ffn_parts(slot_ap, wg, wu, wd):
        g = slot_ap[:, 0:KT * PAIR].rearrange("p (k f) -> p k f", k=KT)
        u = slot_ap[:, KT * PAIR:2 * KT * PAIR].rearrange("p (k f) -> p k f", k=KT)
        d = slot_ap[:, 2 * KT * PAIR:].rearrange("p (r n) -> p r n", n=D)
        return ((g, wg), (u, wu), (d, wd))

    def ffn_weights(b):
        w_in = ins["ffn_w_in"][b["layer"], b["sub"]].rearrange("(k p) f -> p k f", p=P)
        w_out = ins["ffn_w_out"][b["layer"], b["sub"]].rearrange("(i r p) n -> i p r n", p=P, r=2)
        return w_in, w_out

    for b in K.blocks:
        n0 = b["fill0"]
        if b["kind"] == "ffn":
            w_in, w_out = ffn_weights(b)
            for i in range(RING):
                n = n0 + i
                parts = ffn_parts(slot_view(n % RING), w_in[:, :, i * PAIR:(i + 1) * PAIR],
                                  w_in[:, :, DFF + i * PAIR:DFF + (i + 1) * PAIR], w_out[i])
                wait_free(n)
                for j, (dst, src) in enumerate(parts):
                    wait_landed(j, n)
                    sp.dma_start(dst, src).then_inc(K.sem_raw[j], 16)
            split0 = K.fills[n0][1]
            up = 1 if n0 == 0 else 0
            with sp.Fori(RING + up, NPAIR + up) as j1:
                i = j1 - up
                slot = sp.snap((j1 + (n0 - up)) % RING)
                col = sp.snap(i * PAIR)
                landed = sp.snap((j1 + (n0 - up)) * 16)
                freed = sp.snap(j1 * 2 + 2 * (split0 - RING + 1 - up))
                dst = K.raw[:, bass.ds(slot, 1), :].rearrange("p a s -> p (a s)")
                parts = ffn_parts(dst, w_in[:, :, bass.ds(col, PAIR)],
                                  w_in[:, :, bass.ds(col + DFF, PAIR)],
                                  w_out[bass.ds(i, 1)].rearrange("a p r n -> p (a r) n"))
                sp.wait_ge(K.sem.dn_lo, freed)
                for j, (dst, src) in enumerate(parts):
                    sp.wait_ge(K.sem_raw[j], landed)
                    sp.dma_start(dst, src).then_inc(K.sem_raw[j], 16)
        elif b["kind"] == "moe":
            w1 = ins["w1_2"][0].rearrange("e (k p) f -> e p k f", p=P)
            w3 = ins["w3_2"][0].rearrange("e (k p) f -> e p k f", p=P)
            w2 = ins["w2_2"][0].rearrange("e (h r p) n -> e h p r n", p=P, r=2)
            for i in range(4):
                e, h = i // 2, i % 2
                n = n0 + i
                parts = ffn_parts(slot_view(n % RING), w1[e, :, :, h * PAIR:(h + 1) * PAIR],
                                  w3[e, :, :, h * PAIR:(h + 1) * PAIR], w2[e, h])
                wait_free(n)
                for j, (dst, src) in enumerate(parts):
                    wait_landed(j, n)
                    sp.dma_start(dst, src).then_inc(K.sem_raw[j], 16)
            split0 = K.fills[n0][1]
            with sp.Fori(2, NEXP) as e:
                for h in range(2):
                    slot = sp.snap((e * 2 + (n0 + h)) % RING)
                    landed = sp.snap((e * 2 + (n0 + h)) * 16)
                    freed = sp.snap(e * 4 + 2 * (split0 + h - RING + 1))
                    dst = K.raw[:, bass.ds(slot, 1), :].rearrange("p a s -> p (a s)")
                    parts = ffn_parts(
                        dst, w1[bass.ds(e, 1), :, :, h * PAIR:(h + 1) * PAIR].rearrange("e p k f -> p (e k) f"),
                        w3[bass.ds(e, 1), :, :, h * PAIR:(h + 1) * PAIR].rearrange("e p k f -> p (e k) f"),
                        w2[bass.ds(e, 1), h].rearrange("e p r n -> p (e r) n"))
                    sp.wait_ge(K.sem.dn_lo, freed)
                    for j, (dst, src) in enumerate(parts):
                        sp.wait_ge(K.sem_raw[j], landed)
                        sp.dma_start(dst, src).then_inc(K.sem_raw[j], 16)
        else:
            for f, load in enumerate(b["loads"]):
                n = n0 + f
                wait_free(n)
                for j, (dst, src) in enumerate(mixer_parts(K, load, slot_view(n % RING))):
                    wait_landed(j, n)
                    sp.dma_start(dst, src).then_inc(K.sem_raw[j], 16)


def mixer_parts(K, load, slot):
    cuts = [(0, 3), (3, 6), (6, 8)]
    if load[0] == "cols":
        _, w, ranges = load
        total = sum(n for _, n in ranges)
        view = slot[:, 0:KT * total].rearrange("p (k f) -> p k f", k=KT)
        src = w.rearrange("(k p) f -> p k f", p=P)
        (c, n), = ranges
        return [(view[:, a:b, :], src[:, a:b, c:c + n]) for a, b in cuts]
    _, w, r0, nr = load
    width = w.shape[1]
    view = slot[:, 0:nr * width].rearrange("p (r f) -> p r f", r=nr)
    src = w.rearrange("(r p) f -> p r f", p=P)
    third = [(0, nr // 3), (nr // 3, 2 * nr // 3), (2 * nr // 3, nr)]
    return [(view[:, a:b, :], src[:, r0 + a:r0 + b, :]) for a, b in third]


def store_x(K, sp):
    sp.wait_ge(K.sem.post_used, NT * len(K.blocks))
    sp.dma_start(K.out[0].rearrange("(a p) d -> p a d", p=P), K.x[:, :, :]).then_inc(K.sem.out_done, 16)
    sp.wait_ge(K.sem.out_done, 16)


def dve_rstd(K, dve, dst, ss, inv_n, factor=1.0):
    nc = K.nc
    n = ss.shape[1]
    v, y, t = (K.nt[:, i, 0:n] for i in range(3))

    def link(i):
        K.link(dve, "dve", i)

    link(nc.vector.tensor_scalar(v, ss, inv_n, EPS, ALU.mult, ALU.add))
    link(nc.vector.tensor_scalar(y.bitcast(I32), v.bitcast(I32), 1, None, ALU.arith_shift_right))
    link(nc.vector.tensor_scalar(y.bitcast(I32), y.bitcast(I32), -1.0, float(RSQRT_MAGIC), ALU.mult, ALU.add))
    for i in range(3):
        link(nc.vector.tensor_tensor(t, y, y, ALU.mult))
        link(nc.vector.scalar_tensor_tensor(out=t, in0=t, scalar=-0.5, in1=v, op0=ALU.mult, op1=ALU.mult))
        link(nc.vector.scalar_tensor_tensor(out=dst if i == 2 and factor == 1.0 else y, in0=t, scalar=1.5,
                                            in1=y, op0=ALU.add, op1=ALU.mult))
    if factor != 1.0:
        link(nc.vector.tensor_scalar(dst, y, factor, None, ALU.mult))


def pool_power(K, pool, b, where):
    n = b["n"]
    if where == "post" and not has_post(b):
        return
    count, o = ss_count(K, n, where), 4 if where == "post" else 0
    for a in range(NT):
        pool.wait_ge(K.sem.ss_done, count + a + 1)
        v = K.st[:, 8 + o + a:9 + o + a]
        K.nc.gpsimd.tensor_scalar(v, K.st[:, o + a:o + a + 1], 1.0 / D, EPS, ALU.mult, ALU.add)\
            .then_inc(K.sem.mean_sq, 1)
        pool.wait_ge(K.sem.mean_sq, count + a + 1)
        K.nc.gpsimd.tensor_tensor(K.st[:, 2 + o + a:3 + o + a], v, K.minus_half, ALU.pow)\
            .then_inc(K.sem.power, 1)


def has_post(b):
    return b["kind"] not in ("H", "moe")


def act_prenorm(K, act, b):
    n = b["n"]
    for a in range(NT):
        if n:
            act.wait_ge(K.sem.post_used, NT * (n - 1) + a + 1)
        elif a == 0:
            act.wait_ge(K.sem.x_in, 16)
        K.nc.scalar.activation(K.xs[:, a, :], K.x[:, a, :], ACT.Square,
                               accum_out=K.st[:, a:a + 1]).then_inc(K.sem.ss_done, 1)


def dve_prenorm(K, dve, b):
    n = b["n"]
    g = 2 * n
    dve.wait_ge(K.sem_gain[0], 16 * (n + 1))
    for a in range(NT):
        dve.wait_ge(K.sem.power, ss_count(K, n, "pre") + a + 1)
        K.nc.vector.scalar_tensor_tensor(out=K.xs[:, a, :], in0=K.x[:, a, :], scalar=K.st[:, 2 + a:3 + a],
                                         in1=K.gain[0][:, :], op0=ALU.mult, op1=ALU.mult)\
            .then_inc(K.sem.xs_ready, 1)


def ss_count(K, n, where):
    c = 0
    for b in K.blocks[:n]:
        c += NT * (2 if has_post(b) else 1)
    return c + (NT if where == "post" else 0)


def pe_transposes(K, pe, b):
    n = b["n"]
    if n == 0:
        pe.wait_ge(K.sem.consts_in, 16)
    for a in range(NT):
        pe.wait_ge(K.sem.xs_ready, NT * n + a + 1)
        for k in range(KT):
            ins = K.nc.tensor.transpose(K.psum[:, 2 * a + k // 4, (k % 4) * P:(k % 4 + 1) * P],
                                        K.xs[:, a, k * P:(k + 1) * P], K.ident)
        ins.then_inc(K.sem.tr_done, 1)


def turned(K, a, k0, k1):
    return K.psum[:, 2 * a:2 * a + 2, :].rearrange("p b (k s) -> p (b k) s", s=P)[:, k0:k1, :]


def act_hT(K, act, b):
    for a in range(NT):
        act.wait_ge(K.sem.tr_done, NT * b["n"] + a + 1)
        sl = slice(a * P, (a + 1) * P)
        if b["kind"] in ("ffn", "moe"):
            ins = K.nc.scalar.activation(K.hT_hi[:, :, sl], turned(K, a, 0, KT), ACT.Copy)
        else:
            ins = K.nc.scalar.activation(K.hT[:, 0:4, sl], turned(K, a, 0, 4), ACT.Copy)
        ins.then_inc(K.sem.hT_act, 1)


def dve_hT(K, dve, b):
    for a in range(NT):
        sl = slice(a * P, (a + 1) * P)
        if b["kind"] in ("ffn", "moe"):
            dve.wait_ge(K.sem.hT_act, NT * b["n"] + a + 1)
            ins = K.nc.vector.tensor_tensor(K.hT_lo[:, :, sl], turned(K, a, 0, KT),
                                            K.hT_hi[:, :, sl].bitcast(F32), ALU.subtract)
        else:
            dve.wait_ge(K.sem.tr_done, NT * b["n"] + a + 1)
            ins = K.nc.vector.tensor_copy(K.hT[:, 4:KT, sl], turned(K, a, 4, KT))
        ins.then_inc(K.sem.hT_dve, 1)


def act_postnorm(K, act, b):
    if not has_post(b):
        return
    for a in range(NT):
        act.wait_ge(K.sem.y_done, NT * b["n"] + a + 1)
        K.nc.scalar.activation(K.xs[:, a, :], K.psum[:, 2 * a:2 * a + 2, :].rearrange("p h n -> p (h n)"),
                               ACT.Square, accum_out=K.st[:, 4 + a:5 + a]).then_inc(K.sem.ss_done, 1)


def dve_postnorm(K, dve, b):
    n = b["n"]
    if has_post(b):
        dve.wait_ge(K.sem_gain[1], 16 * (n + 1))
        for a in range(NT):
            dve.wait_ge(K.sem.power, ss_count(K, n, "post") + a + 1)
            y = K.psum[:, 2 * a:2 * a + 2, :].rearrange("p h n -> p (h n)")
            K.link(dve, "dve", K.nc.vector.scalar_tensor_tensor(
                out=K.xs[:, a, :], in0=y, scalar=K.st[:, 6 + a:7 + a], in1=K.gain[1][:, :],
                op0=ALU.mult, op1=ALU.mult))
            K.nc.vector.scalar_tensor_tensor(
                out=K.x[:, a, :], in0=K.xs[:, a, :], scalar=0.5 if b["kind"] == "ffn" else 1.0,
                in1=K.x[:, a, :], op0=ALU.mult, op1=ALU.add).then_inc(K.sem.post_used, 1)
    else:
        for a in range(NT):
            dve.wait_ge(K.sem.y_done, NT * n + a + 1)
            y = K.psum[:, 2 * a:2 * a + 2, :].rearrange("p h n -> p (h n)")
            K.nc.vector.tensor_tensor(K.x[:, a, :], K.x[:, a, :], y, ALU.add).then_inc(K.sem.post_used, 1)


def pool_gains(K, pool, b):
    n = b["n"]
    nc = K.nc
    if n:
        pool.wait_ge(K.sem.post_used, NT * n)
    nc.gpsimd.dma_start(K.gain[1][:, :], K.gains[2 * n + 1].to_broadcast([P, D])).then_inc(K.sem_gain[1], 16)
    if n + 1 < len(K.blocks):
        pool.wait_ge(K.sem.xs_ready, NT * (n + 1))
        nc.gpsimd.dma_start(K.gain[0][:, :], K.gains[2 * n + 2].to_broadcast([P, D])).then_inc(K.sem_gain[0], 16)


def raw_gu(K, slot, t):
    r = K.raw[:, slot, :] if isinstance(slot, int) else K.raw[:, bass.ds(slot, 1), :].rearrange("p a s -> p (a s)")
    return r[:, 0:2 * KT * PAIR].rearrange("p (k f) -> p k f", f=PAIR)[:, :, t * P:(t + 1) * P]


def raw_dn(K, slot, t):
    r = K.raw[:, slot, :] if isinstance(slot, int) else K.raw[:, bass.ds(slot, 1), :].rearrange("p a s -> p (a s)")
    o = 2 * KT * PAIR + t * D
    return r[:, o:o + D]


def early_split(K, b):
    return b["kind"] in ("ffn", "moe") and b["n"] > 0 and K.blocks[b["n"] - 1]["kind"] != "H"


def late_second(K, b):
    return K.blocks[b["n"] - 1]["kind"] in ("ffn", "moe")


def act_split_gu(K, act, t, slot, landed):
    act.wait_ge(K.sem_raw[0], landed)
    act.wait_ge(K.sem_raw[1], landed)
    K.nc.scalar.activation(K.gu_hi[:, t, :, :], raw_gu(K, slot, t), ACT.Copy).then_inc(K.sem.gu_hi, 1)


def act_split_dn(K, act, t, slot, landed, dn_free):
    act.wait_ge(K.sem_raw[2], landed)
    if dn_free is not None:
        act.wait_ge(K.sem.down_done, dn_free)
    K.nc.scalar.activation(K.dn_hi[:, t, :], raw_dn(K, slot, t), ACT.Copy).then_inc(K.sem.dn_hi, 1)


def dve_lo_gu(K, dve, t, slot, done):
    dve.wait_ge(K.sem.gu_hi, done)
    K.nc.vector.tensor_tensor(K.gu_lo[:, t, :, :], raw_gu(K, slot, t), K.gu_hi[:, t, :, :].bitcast(F32),
                              ALU.subtract).then_inc(K.sem.gu_lo, 1)


def dve_lo_dn(K, dve, t, slot, done):
    dve.wait_ge(K.sem.dn_hi, done)
    K.nc.vector.tensor_tensor(K.dn_lo[:, t, :], raw_dn(K, slot, t), K.dn_hi[:, t, :].bitcast(F32),
                              ALU.subtract).then_inc(K.sem.dn_lo, 1)


def act_first_splits(K, act, b, part):
    F0, T0 = b["fill0"], b["tile0"]
    slot, landed = F0 % RING, 16 * (F0 + 1)
    second = late_second(K, b) if early_split(K, b) else True
    if part == 0:
        if late_second(K, b):
            act.wait_ge(K.sem.gu_done, T0)
        else:
            p = K.blocks[b["n"] - 1]
            act.wait_ge(K.sem.oT_sb, p["out0"] + NT * len(p["attn"].quads))
        act_split_gu(K, act, 0, slot, landed)
        act_split_dn(K, act, 0, slot, landed, T0 - 1 if late_second(K, b) else None)
    if (part == 1) == second:
        act_split_gu(K, act, 1, slot, landed)


def dve_first_splits(K, dve, b, part):
    F0, T0 = b["fill0"], b["tile0"]
    slot = F0 % RING
    second = late_second(K, b) if early_split(K, b) else True
    if part == 0:
        dve_lo_gu(K, dve, 0, slot, T0 + 1)
        dve_lo_dn(K, dve, 0, slot, T0 + 1)
    if (part == 1) == second:
        dve_lo_gu(K, dve, 1, slot, T0 + 2)


def act_ffn(K, act, b):
    nc, T0, F0, n = K.nc, b["tile0"], b["fill0"], b["n"]

    def split_gu(t, slot, landed, gu_free):
        act_split_gu(K, act, t, slot, landed)

    def split_dn(t, slot, landed, dn_free):
        act_split_dn(K, act, t, slot, landed, dn_free)

    def silu(t, done):
        act.wait_ge(K.sem.gu_done, done)
        nc.scalar.activation(K.sg[:, t, :], K.psum[:, 4 + t, 0:SEQ], ACT.Silu).then_inc(K.sem.silu, 1)

    s0, s1 = F0 % RING, (F0 + 1) % RING
    if not early_split(K, b):
        if n:
            act.wait_ge(K.sem.y_done, NT * n)
        split_gu(0, s0, 16 * (F0 + 1), None)
        split_dn(0, s0, 16 * (F0 + 1), None)
        split_gu(1, s0, 16 * (F0 + 1), None)
    silu(0, T0 + 1)
    split_gu(0, s1, 16 * (F0 + 2), None)
    split_dn(1, s0, 16 * (F0 + 1), None)
    silu(1, T0 + 2)
    split_gu(1, s1, 16 * (F0 + 2), None)
    split_dn(0, s1, 16 * (F0 + 2), T0 + 1)
    with act.Fori(1, b["pairs"] - 1) as i:
        cur = act.snap((i + F0) % RING)
        nxt = act.snap((i + (F0 + 1)) % RING)
        here = act.snap((i + (F0 + 1)) * 16)
        there = act.snap((i + (F0 + 2)) * 16)
        t1 = act.snap(i * 2 + (T0 + 1))
        t2 = act.snap(i * 2 + (T0 + 2))
        t0 = act.snap(i * 2 + T0)
        silu(0, t1)
        split_gu(0, nxt, there, None)
        split_dn(1, cur, here, t0)
        silu(1, t2)
        split_gu(1, nxt, there, None)
        split_dn(0, nxt, there, t1)
    last = b["pairs"] - 1
    silu(0, T0 + 2 * last + 1)
    split_dn(1, (F0 + last) % RING, 16 * (F0 + last + 1), T0 + 2 * last)
    silu(1, T0 + 2 * last + 2)


def dve_ffn(K, dve, b):
    nc, T0, F0 = K.nc, b["tile0"], b["fill0"]
    moe = b["kind"] == "moe"

    def lo_gu(t, slot, done):
        dve_lo_gu(K, dve, t, slot, done)

    def lo_dn(t, slot, done):
        dve_lo_dn(K, dve, t, slot, done)

    def times_up(t, done, mine, expert):
        dve.wait_ge(K.sem.silu, done)
        if moe:
            w = K.comb_bc[:, expert, :] if isinstance(expert, int) else \
                K.comb_bc[:, bass.ds(expert, 1), :].rearrange("p a s -> p (a s)")
            nc.vector.tensor_tensor(K.sg[:, t, :], K.sg[:, t, :], w, ALU.mult).then_inc(K.sem.sgc, 1)
            dve.wait_ge(K.sem.sgc, mine)
        nc.vector.tensor_tensor(K.hid[:, t, :], K.sg[:, t, :], K.psum[:, 4 + t, SEQ:2 * SEQ],
                                ALU.mult).then_inc(K.sem.hid_done, 1)

    def lo_hid(t, done):
        dve.wait_ge(K.sem.hid_hi, done)
        nc.vector.tensor_tensor(K.hid_lo[:, t, :], K.hid[:, t, :], K.hid_hi[:, t, :].bitcast(F32),
                                ALU.subtract).then_inc(K.sem.hid_lo, 1)

    s0, s1 = F0 % RING, (F0 + 1) % RING
    if not early_split(K, b):
        lo_gu(0, s0, T0 + 1)
        lo_dn(0, s0, T0 + 1)
        lo_gu(1, s0, T0 + 2)
    times_up(0, T0 + 1, 1, 0)
    lo_hid(0, T0 + 1)
    lo_gu(0, s1, T0 + 3)
    lo_dn(1, s0, T0 + 2)
    times_up(1, T0 + 2, 2, 0)
    lo_hid(1, T0 + 2)
    lo_gu(1, s1, T0 + 4)
    lo_dn(0, s1, T0 + 3)

    def pair(cur, nxt, T, mine, expert):
        for t in range(2):
            times_up(t, T + t, mine + t, expert)
            lo_hid(t, T + t)
            lo_gu(t, nxt, T + t + 2)
            lo_dn(1 - t, cur if t == 0 else nxt, T + t + 1)

    last = b["pairs"] - 1
    if moe:
        pair(s1, (F0 + 2) % RING, T0 + 3, 3, 0)
        with dve.Fori(1, NEXP - 1) as e:
            for h in range(2):
                pair(dve.snap((e * 2 + (F0 + h)) % RING), dve.snap((e * 2 + (F0 + h + 1)) % RING),
                     e * 4 + (T0 + 2 * h + 1), e * 4 + (2 * h + 1), e)
        pair((F0 + last - 1) % RING, (F0 + last) % RING, T0 + 2 * last - 1, 2 * last - 1, NEXP - 1)
    else:
        with dve.Fori(1, last) as i:
            pair(dve.snap((i + F0) % RING), dve.snap((i + (F0 + 1)) % RING), i * 2 + (T0 + 1), 0, 0)
    L = 2 * last
    times_up(0, T0 + L + 1, L + 1, NEXP - 1)
    lo_hid(0, T0 + L + 1)
    lo_dn(1, (F0 + last) % RING, T0 + L + 2)
    times_up(1, T0 + L + 2, L + 2, NEXP - 1)
    lo_hid(1, T0 + L + 2)


def pool_ffn(K, pool, b):
    nc, T0 = K.nc, b["tile0"]

    def high(t, done, dn_free):
        pool.wait_ge(K.sem.hid_done, done)
        if dn_free is not None:
            pool.wait_ge(K.sem.down_done, dn_free)
        nc.gpsimd.tensor_tensor(K.hid_hi[:, t, :], K.hid[:, t, :], K.one.to_broadcast([P, SEQ]), ALU.mult)\
            .then_inc(K.sem.hid_hi, 1)

    high(0, T0 + 1, None)
    high(1, T0 + 2, None)
    with pool.Fori(1, b["pairs"]) as i:
        t0, tm, t1, t2 = (pool.snap(i * 2 + (T0 + k)) for k in (0, -1, 1, 2))
        high(0, t1, tm)
        high(1, t2, t0)


def pe_ffn(K, pe, b):
    nc, T0 = K.nc, b["tile0"]
    def gate_up(t, lo_done, bank_free, start=False):
        pe.wait_ge(K.sem.gu_lo, lo_done)
        if bank_free is not None:
            pe.wait_ge(K.sem.hid_done, bank_free)
        for part in range(2):
            out = K.psum[:, 4 + t, part * SEQ:(part + 1) * SEQ]
            for k in range(KT):
                if start and part == 0 and k == 0:
                    pe.wait_ge(K.sem.hT_dve, NT * (b["n"] + 1))
                w_hi, w_lo = K.gu_hi[:, t, part * KT + k, :], K.gu_lo[:, t, part * KT + k, :]
                nc.tensor.matmul(out, w_hi, K.hT_hi[:, k, :], start=k == 0, stop=False)
                nc.tensor.matmul(out, w_hi, K.hT_lo[:, k, :], start=False, stop=False)
                ins = nc.tensor.matmul(out, w_lo, K.hT_hi[:, k, :], start=False, stop=k == KT - 1)
        ins.then_inc(K.sem.gu_done, 1)

    def down(t, lo_done, first=False, last=False):
        pe.wait_ge(K.sem.dn_lo, lo_done)
        pe.wait_ge(K.sem.hid_lo, lo_done)
        for a in range(NT):
            h_hi, h_lo = (h[:, t, a * P:(a + 1) * P] for h in (K.hid_hi, K.hid_lo))
            for half in range(2):
                out = K.psum[:, 2 * a + half, :]
                d_hi, d_lo = (d[:, t, half * 512:(half + 1) * 512] for d in (K.dn_hi, K.dn_lo))
                nc.tensor.matmul(out, h_hi, d_hi, start=first, stop=False)
                nc.tensor.matmul(out, h_hi, d_lo, start=False, stop=False)
                ins = nc.tensor.matmul(out, h_lo, d_hi, start=False, stop=last)
            if last:
                ins.then_inc(K.sem.y_done, 1)
        if not last:
            ins.then_inc(K.sem.down_done, 1)

    gate_up(0, T0 + 1, None, start=True)
    gate_up(1, T0 + 2, None)
    down(0, T0 + 1, first=True)
    with pe.Fori(0, b["pairs"] - 1) as i:
        t1, t2, t3, t4 = (pe.snap(i * 2 + (T0 + k)) for k in (1, 2, 3, 4))
        gate_up(0, t3, t1)
        down(1, t2)
        gate_up(1, t4, t2)
        down(0, t3)
    down(1, T0 + b["tiles"], last=True)
    pe.wait_ge(K.sem.y_done, NT * (b["n"] + 1))
    pe.nop().then_inc(K.sem.down_done, 1)


PROJ_BANKS = (4, 5, 6, 7)


def pe_projections(K, pe, b):
    nc = K.nc
    pe.wait_ge(K.sem.hT_dve, 2 * (b["n"] + 1))
    pe.wait_ge(K.sem.hT_act, 2 * (b["n"] + 1))
    seen = -1
    for q, it in enumerate(b["items"]):
        g = b["item0"] + q
        f = it["fill"]
        slot, landed = K.fill_of(b, f)
        if f != seen:
            for j in range(3):
                pe.wait_ge(K.sem_raw[j], landed)
            seen = f
        if q >= 4:
            pe.wait_ge(K.sem.evac_act if (q - 4) % 2 == 0 else K.sem.evac_dve, evac_count(K, b, q - 4))
        total = sum(n for _, n in b["loads"][f][2])
        w = K.raw[:, slot, 0:KT * total].rearrange("p (k f) -> p k f", k=KT)
        bank = PROJ_BANKS[q % 4]
        for k in range(KT):
            if it["form"] == "T":
                ins = nc.tensor.matmul(K.psum[:, bank, 0:SEQ], w[:, k, it["c0"]:it["c0"] + P], K.hT[:, k, :],
                                       start=k == 0, stop=k == KT - 1)
            else:
                a = it["a"]
                row = it.get("row")
                if row is not None and k == 0:
                    if row == 0 and a == 0:
                        pe.wait_ge(K.sem.h_rows, 32)
                    nc.tensor.matmul(K.psum[:, bank, 0:it["n"]], K.c2[0:1, C_ONES - C_FIRST:C_ONES - C_FIRST + P],
                                     K.bgrow[0:1, row:row + it["n"]], start=True, stop=False)
                ins = nc.tensor.matmul(K.psum[:, bank, 0:it["n"]], K.hT[:, k, a * P:(a + 1) * P],
                                       w[:, k, it["c0"]:it["c0"] + it["n"]], start=k == 0 and row is None,
                                       stop=k == KT - 1)
        ins.then_inc(K.sem.proj, 1)
        if q + 1 == len(b["items"]) or b["items"][q + 1]["fill"] != f:
            pe.wait_ge(K.sem.proj, g + 1)
            pe.nop().then_inc(K.sem.slots_used, 1)


def evac_count(K, b, q):
    c = 0
    for o in K.blocks[:b["n"]]:
        m = len(o.get("items", ()))
        c += (m + 1) // 2 if q % 2 == 0 else m // 2
    return c + q // 2 + 1


def evacuate(K, eng, b, parity):
    nc = K.nc
    sem = K.sem.evac_act if parity == 0 else K.sem.evac_dve

    def copy(dst, src):
        if parity == 0:
            return nc.scalar.activation(dst, src, ACT.Copy)
        return nc.vector.tensor_copy(dst, src)

    for q, it in enumerate(b["items"]):
        if q % 2 != parity:
            continue
        eng.wait_ge(K.sem.proj, b["item0"] + q + 1)
        bank = PROJ_BANKS[q % 4]
        if it.get("zc") is not None:
            kv, c = it["zc"]
            for h in range(2):
                src = K.psum[h * HD:(h + 1) * HD, bank, 0:SEQ]
                copy(K.zc[0:HD, kv, 2 * c + h, :], src)
                ins = copy(K.zc[HD:P, kv, 2 * c + h, 0:SEQ - 1], src[:, 1:SEQ])
        elif it.get("both") is not None:
            for h in range(2):
                for to in range(2):
                    ins = copy(K.kT[to * HD:(to + 1) * HD, it["both"] + h, :],
                               K.psum[h * HD:(h + 1) * HD, bank, 0:SEQ])
        elif it["form"] == "T":
            ins = copy(it["dst"], K.psum[:, bank, 0:SEQ])
        else:
            ins = copy(it["dst"], K.psum[:, bank, 0:it["n"]])
        ins.then_inc(sem, 1)


def wait_projected(K, eng, b):
    m = len(b["items"])
    eng.wait_ge(K.sem.evac_act, evac_count(K, b, (m - 1) // 2 * 2))
    eng.wait_ge(K.sem.evac_dve, evac_count(K, b, (m - 2) // 2 * 2 + 1))


def units_of(b):
    att = b["attn"]
    streams = (0, 1, 2) if b["kind"] == "B" else (0,)
    units, si, q = [], 0, 0
    for a in range(NT):
        for quad in att.quads:
            for s in streams:
                scored = s < 2
                units.append(dict(a=a, quad=quad, s=s, si=si if scored else None, q=q, u=len(units),
                                  first=s == 0, last=s == streams[-1],
                                  nk=N_CMP if not scored else SEQ if b["kind"] == "H" else P * (a + 1)))
                si += scored
            q += 1
    return units


def scored_units(b):
    return [u for u in b["units"] if u["si"] is not None]


def pe_attention(K, pe, b):
    nc, att, kind = K.nc, b["attn"], b["kind"]
    U0, S0, Q0 = b["unit0"], b["sunit0"], b["out0"]
    scored = scored_units(b)

    def scores(i):
        x = scored[i]
        if i >= 2:
            pe.wait_ge(K.sem.sbias, S0 + i - 1)
        for t in range(2):
            for half in range(2):
                hs = slice(half * HD, (half + 1) * HD)
                ins = nc.tensor.matmul(K.psum[:, 2 * (i % 2) + half, t * SEQ:t * SEQ + x["nk"]],
                                       K.qT[hs, 2 * x["quad"] + t, x["a"] * P:(x["a"] + 1) * P],
                                       K.kT[hs, att.ktile(x["quad"], t, x["s"]), 0:x["nk"]],
                                       start=True, stop=True)
        ins.then_inc(K.sem.scores, 1)

    def transposes(x):
        u, h0 = x["u"], 4 * x["quad"]
        if x["si"] is not None:
            pe.wait_ge(K.sem.psc, S0 + x["si"] + 1)
        if u >= 1:
            pe.wait_ge(K.sem.pT_sb, U0 + u)
        if x["si"] is None:
            for r in range(4):
                ins = nc.tensor.transpose(K.psum[0:N_CMP, 4, r * P:(r + 1) * P],
                                          K.pc[:, x["a"], h0 + r, :], K.ident)
        else:
            for j in range(x["nk"] // P):
                for r in range(4):
                    ins = nc.tensor.transpose(K.psum[:, 4 + j, r * P:(r + 1) * P],
                                              K.S[:, x["si"] % 2, r, j * P:(j + 1) * P], K.ident)
        ins.then_inc(K.sem.pT, 1)

    def values(x):
        u, q, quad = x["u"], x["q"], x["quad"]
        pe.wait_ge(K.sem.pT_sb, U0 + u + 1)
        if x["first"] and q >= 2:
            pe.wait_ge(K.sem.oT_sb, Q0 + q - 1)
        bank, nj = 6 + q % 2, x["nk"] // P
        for half in range(2):
            out = K.psum[half * HD:(half + 1) * HD, bank, 0:2 * P]

            def probs(j, n=P):
                return K.PT[0:n, u % 2, j, half * 2 * P:(half + 1) * 2 * P]

            if x["si"] is None:
                ins = nc.tensor.matmul(out, K.vcb[0:N_CMP, quad, :], probs(0, N_CMP), start=False, stop=True)
            elif att.gqa:
                v0 = att.vcol(quad, half, x["s"])
                for j in range(nj):
                    ins = nc.tensor.matmul(out, K.v[:, j, v0:v0 + HD], probs(j),
                                           start=j == 0 and x["first"], stop=j == nj - 1 and x["last"])
            else:
                for t in range(2):
                    v0 = att.vcol(quad, 2 * t + half, 0)
                    for j in range(nj):
                        ins = nc.tensor.matmul(out[:, t * P:(t + 1) * P], K.v[:, j, v0:v0 + HD],
                                               probs(j)[:, t * P:(t + 1) * P],
                                               start=j == 0, stop=j == nj - 1)
        ins.then_inc(K.sem.oPV, 1)

    wait_projected(K, pe, b)
    if kind == "B":
        pe.wait_ge(K.sem.pc, NT)
    if kind == "H":
        pe.wait_ge(K.sem.h_qT, 1)
        pe.wait_ge(K.sem.h_kT, 1)
    scores(0)
    scores(1)
    for x in b["units"]:
        if x["si"] is not None and x["si"] + 2 < len(scored):
            scores(x["si"] + 2)
        transposes(x)
        values(x)


def dve_attention(K, dve, b):
    nc, att, kind = K.nc, b["attn"], b["kind"]
    U0, S0, Q0 = b["unit0"], b["sunit0"], b["out0"]
    scored = scored_units(b)

    def head_slice(x):
        return slice(4 * x["quad"], 4 * x["quad"] + 4)

    def biased(i):
        x = scored[i]
        nk, hs = x["nk"], head_slice(x)
        src = K.psum[:, 2 * (i % 2):2 * (i % 2) + 2, :].rearrange("p b (h k) -> p (b h) k", h=2)[:, :, 0:nk]
        dst = K.S[:, i % 2, :, 0:nk]
        dve.wait_ge(K.sem.scores, S0 + i + 1)
        if i >= 2:
            dve.wait_ge(K.sem.pT, U0 + scored[i - 2]["u"] + 1)
        if kind == "H":
            nc.vector.tensor_scalar(dst, src, SCALE, None, ALU.mult).then_inc(K.sem.sbias, 1)
        elif kind == "A" and x["a"] == 1:
            nc.vector.scalar_tensor_tensor(out=dst[:, :, 0:P], in0=src[:, :, 0:P], scalar=SCALE,
                                           in1=K.biasA[:, hs, :], op0=ALU.mult, op1=ALU.add)
            nc.vector.scalar_tensor_tensor(out=dst[:, :, P:], in0=src[:, :, P:], scalar=SCALE,
                                           in1=K.bias[:, hs, P:], op0=ALU.mult, op1=ALU.add)\
                .then_inc(K.sem.sbias, 1)
        else:
            nc.vector.scalar_tensor_tensor(out=dst, in0=src, scalar=SCALE, in1=K.bias[:, hs, SEQ - nk:],
                                           op0=ALU.mult, op1=ALU.add).then_inc(K.sem.sbias, 1)
        dve.wait_ge(K.sem.sbias, S0 + i + 1)
        m = K.am[:, i % 2, :]
        K.link(dve, "dve", nc.vector.tensor_reduce(out=m, in_=dst, axis=AX, op=ALU.max))
        if kind == "A":
            K.link(dve, "dve", nc.vector.tensor_tensor(m, m, K.sink[:, b["j"], hs], ALU.max))
            K.link(dve, "dve", nc.vector.tensor_tensor(K.se[:, i % 2, :], K.sink[:, b["j"], hs], m, ALU.subtract))
        nc.vector.tensor_scalar(m, m, -1.0, None, ALU.mult).then_inc(K.sem.smax, 1)

    def coefficients(i):
        x = scored[i]
        dve.wait_ge(K.sem.sexp, S0 + i + 1)
        d, co = K.den[:, i % 2, :], K.coef[:, i % 2, :]
        if kind == "A":
            K.link(dve, "dve", nc.vector.tensor_tensor(d, d, K.se[:, i % 2, :], ALU.add))
        K.link(dve, "dve", nc.vector.tensor_scalar(d, d, TINY, None, ALU.max))
        if kind == "B":
            h0 = 4 * x["quad"]
            gate = K.bgate[:, x["a"], 3 * h0:3 * h0 + 12].rearrange("p (t h c) -> p h t c", t=2, c=3)
            K.link(dve, "dve", nc.vector.reciprocal(d, d))
            nc.vector.tensor_tensor(co.rearrange("p (h t) -> p h t", h=2), d.rearrange("p (h t) -> p h t", h=2),
                                    gate[:, :, :, 1 + x["s"]], ALU.mult).then_inc(K.sem.coef, 1)
        else:
            nc.vector.reciprocal(co, d).then_inc(K.sem.coef, 1)

    def copy_out(x):
        dve.wait_ge(K.sem.oPV, U0 + x["u"] + 1)
        nc.vector.tensor_copy(K.oT[:, 2 * x["quad"]:2 * x["quad"] + 2, x["a"] * P:(x["a"] + 1) * P],
                              K.psum[:, 6 + x["q"] % 2, 0:2 * P].rearrange("p (t s) -> p t s", t=2))\
            .then_inc(K.sem.oT_sb, 1)

    if kind == "B":
        dve.wait_ge(K.sem.bgate, 1)
    if kind != "H":
        dve.wait_ge(K.sem.bias_turned, len(bias_chunks(K)))
    biased(0)
    biased(1)
    for x in b["units"]:
        if x["si"] is not None:
            coefficients(x["si"])
            if x["si"] + 2 < len(scored):
                biased(x["si"] + 2)
            if kind == "H":
                dve_conv(K, dve, b, range(2 * x["si"], min(2 * x["si"] + 2, CONV_K)))
        if x["u"] >= 1 and b["units"][x["u"] - 1]["last"]:
            copy_out(b["units"][x["u"] - 1])
    copy_out(b["units"][-1])


def act_attention(K, act, b):
    nc, kind = K.nc, b["kind"]
    U0, S0 = b["unit0"], b["sunit0"]
    scored = scored_units(b)

    def exps(i):
        x = scored[i]
        act.wait_ge(K.sem.smax, S0 + i + 1)
        for r in range(4):
            s = K.S[:, i % 2, r, 0:x["nk"]]
            ins = nc.scalar.activation(s, s, ACT.Exp, bias=K.am[:, i % 2, r:r + 1],
                                       accum_out=K.den[:, i % 2, r:r + 1])
        if kind == "A":
            ins = nc.scalar.activation(K.se[:, i % 2, :], K.se[:, i % 2, :], ACT.Exp)
        ins.then_inc(K.sem.sexp, 1)

    def copy_pT(x):
        u = x["u"]
        act.wait_ge(K.sem.pT, U0 + u + 1)
        if u >= 2:
            act.wait_ge(K.sem.oPV, U0 + u - 1)
        if x["si"] is None:
            ins = nc.scalar.activation(K.PT[0:N_CMP, u % 2, 0, :], K.psum[0:N_CMP, 4, :], ACT.Copy)
        else:
            nj = x["nk"] // P
            ins = nc.scalar.activation(K.PT[:, u % 2, 0:nj, :], K.psum[:, 4:4 + nj, :], ACT.Copy)
        ins.then_inc(K.sem.pT_sb, 1)

    exps(0)
    exps(1)
    for x in b["units"]:
        copy_pT(x)
        if x["si"] is not None and x["si"] + 2 < len(scored):
            exps(x["si"] + 2)


def pool_attention(K, pool, b):
    S0 = b["sunit0"]
    for i, x in enumerate(scored_units(b)):
        pool.wait_ge(K.sem.coef, S0 + i + 1)
        s = K.S[:, i % 2, :, 0:x["nk"]]
        K.nc.gpsimd.tensor_tensor(s, s, K.coef[:, i % 2, :].unsqueeze(2).to_broadcast([P, 4, x["nk"]]),
                                  ALU.mult).then_inc(K.sem.psc, 1)


def pe_output(K, pe, b):
    nc = K.nc
    pe.wait_ge(K.sem.oT_sb, b["out0"] + NT * len(b["attn"].quads))
    lhs = K.hT if b["kind"] == "H" else K.oT
    for c in range(2):
        slot, landed = K.fill_of(b, b["wo_fill"] + c)
        for j in range(3):
            pe.wait_ge(K.sem_raw[j], landed)
        w = K.raw[:, slot, 0:4 * D].rearrange("p (r n) -> p r n", r=4)
        for a in range(NT):
            for r in range(4):
                t = 4 * c + r
                for half in range(2):
                    ins = nc.tensor.matmul(K.psum[:, 2 * a + half, :], lhs[:, t, a * P:(a + 1) * P],
                                           w[:, r, half * 512:(half + 1) * 512], start=t == 0, stop=t == 7)
            if c == 1:
                ins.then_inc(K.sem.y_done, 1)
        if c == 0:
            ins.then_inc(K.sem.slots_used, 1)
    pe.wait_ge(K.sem.y_done, NT * (b["n"] + 1))
    pe.nop().then_inc(K.sem.slots_used, 1)


def bias_chunks(K):
    full = K.bias[:, :, :].rearrange("p h s -> p (h s)")
    window = K.biasA[:, :, :].rearrange("p h s -> p (h s)")
    return [t[:, o:o + 512] for t, n in ((full, NH * SEQ), (window, NH * P)) for o in range(0, n, 512)]


def pe_bias(K, pe, b):
    wait_projected(K, pe, b)
    pe.wait_ge(K.sem.bias_in, 32)
    for i, chunk in enumerate(bias_chunks(K)):
        if i >= 4:
            pe.wait_ge(K.sem.bias_turned, i - 3)
        K.nc.tensor.matmul(K.psum[:, 4 + i % 4, :], K.cst[:, C_REV:C_REV + P], chunk, start=True, stop=True)\
            .then_inc(K.sem.bias_product, 1)
    pe.wait_ge(K.sem.bias_turned, len(bias_chunks(K)))


def act_bias(K, act, b):
    for i, chunk in enumerate(bias_chunks(K)):
        act.wait_ge(K.sem.bias_product, i + 1)
        K.nc.scalar.activation(chunk, K.psum[:, 4 + i % 4, :], ACT.Copy).then_inc(K.sem.bias_turned, 1)


CMP_BANKS = (5, 6, 7, 4)


def pool_compress_loads(K, pool, b):
    nc, ins = K.nc, K.ins
    if b["n"]:
        pool.wait_ge(K.sem.y_done, NT * b["n"])
    with nc.allow_non_contiguous_dma(reason="position table, 2048 elements"):
        for kv in range(2):
            nc.gpsimd.dma_start(K.cpos[:, kv, :], ins["b_cmp_pos"][0, kv].rearrange("(l t) d -> (t d) l", t=2))\
                .then_inc(K.sem.cmp_small, 16)
    for kv in range(2):
        nc.gpsimd.dma_start(K.cw2[:, kv, :, :], ins["b_cmp_w2"][0, kv].rearrange("(j p) d -> p j d", p=P))\
            .then_inc(K.sem.cmp_small, 16)


def dve_compress(K, dve, b):
    nc = K.nc

    def link(i):
        K.link(dve, "dve", i)

    wait_projected(K, dve, b)
    dve.wait_ge(K.sem.cmp_small, 64)
    for kv in range(2):
        z = K.zc[:, kv, :, :]
        src = bass.AP(z.tensor, z.offset, [list(z.ap[0]), [2, CMP_ROW_TILES], [SEQ, G_B], [CMP_STRIDE, N_CMP]])
        pos = K.cpos[:, kv, :].unsqueeze(2).unsqueeze(3).to_broadcast([P, CMP_ROW_TILES, G_B, N_CMP])
        nc.vector.tensor_tensor(K.z2[:, kv, :, :].rearrange("p l (g n) -> p l g n", g=G_B), src, pos, ALU.add)\
            .then_inc(K.sem.z2, 1)
    dve.wait_ge(K.sem.chidT_ps, 1)
    nc.vector.tensor_copy(K.chidT[:, :, :, :].rearrange("p v j n -> p (v j n)"),
                          K.psum[:, 6, 0:4 * G_B * N_CMP]).then_inc(K.sem.chidT, 1)
    dve.wait_ge(K.sem.kcb_ps, 1)
    nc.vector.tensor_copy(K.kcb[:, :], K.psum[:, 7, 0:G_B * N_CMP])
    nc.vector.tensor_copy(K.vcb[0:N_CMP, :, :].rearrange("p g d -> p (g d)"), K.psum[0:N_CMP, 4, 0:G_B * HD])\
        .then_inc(K.sem.kcb, 1)
    for a in range(NT):
        dve.wait_ge(K.sem.s_cmp, a + 1)
        pc = K.pc[:, a, :, :]
        mask = K.cst[:, C_CMPM + a * N_CMP:C_CMPM + (a + 1) * N_CMP].unsqueeze(1).to_broadcast([P, NH, N_CMP])
        ok = K.cst[:, C_CMPOK + a * N_CMP:C_CMPOK + (a + 1) * N_CMP].unsqueeze(1).to_broadcast([P, NH, N_CMP])
        m, d = K.cs[:, 2 * a, :], K.cs[:, 2 * a + 1, :]

        def wide(x):
            return x.unsqueeze(2).to_broadcast([P, NH, N_CMP])

        for half in range(2):
            slots = K.pc[:, a, :, :].rearrange("p (q h t) n -> p q h (t n)", q=4, h=2)[:, :, half, :]
            ps = K.psum[:, CMP_BANKS[2 * a + half], 0:8 * N_CMP].rearrange("p (q c) -> p q c", q=4)
            link(nc.vector.tensor_scalar(slots, ps, SCALE, None, ALU.mult))
        link(nc.vector.tensor_tensor(pc, pc, mask, ALU.add))
        link(nc.vector.tensor_reduce(out=m, in_=pc, axis=AX, op=ALU.max))
        nc.vector.tensor_tensor(pc, pc, wide(m), ALU.subtract).then_inc(K.sem.cmp_arg, 1)
        dve.wait_ge(K.sem.cmp_exp, a + 1)
        link(nc.vector.tensor_tensor(pc, pc, ok, ALU.mult))
        link(nc.vector.tensor_reduce(out=d, in_=pc, axis=AX, op=ALU.add))
        link(nc.vector.tensor_scalar(d, d, TINY, None, ALU.max))
        link(nc.vector.reciprocal(d, d))
        if a == 0:
            dve.wait_ge(K.sem.bgate, 1)
        gate = K.bgate[:, a, :].rearrange("p (q t h c) -> p q h t c", q=4, t=2, c=3)[:, :, :, :, 0]
        dq = d.rearrange("p (q h t) -> p q h t", q=4, h=2)
        link(nc.vector.tensor_tensor(dq, dq, gate, ALU.mult))
        nc.vector.tensor_tensor(pc, pc, wide(d), ALU.mult).then_inc(K.sem.pc, 1)


def act_compress(K, act, b):
    nc = K.nc
    wait_projected(K, act, b)
    g = K.bgate[:, :, :].rearrange("p a c -> p (a c)")
    nc.scalar.activation(g, g, ACT.Sigmoid).then_inc(K.sem.bgate, 1)
    act.wait_ge(K.sem.chid_ps, 1)
    nc.scalar.activation(K.chid[0:G_B * N_CMP, :, :],
                         K.psum[0:G_B * N_CMP, 4:6, 0:SEQ], ACT.Gelu_apprx_tanh).then_inc(K.sem.gelu, 1)
    for a in range(NT):
        act.wait_ge(K.sem.cmp_arg, a + 1)
        pc = K.pc[:, a, :, :]
        nc.scalar.activation(pc, pc, ACT.Exp).then_inc(K.sem.cmp_exp, 1)


def pe_compress(K, pe, b):
    nc, att, M = K.nc, b["attn"], G_B * N_CMP
    for kv in range(2):
        slot, landed = K.fill_of(b, b["w1_fill"] + kv)
        pe.wait_ge(K.sem.z2, kv + 1)
        for j in range(3):
            pe.wait_ge(K.sem_raw[j], landed)
        if kv == 0:
            wait_projected(K, pe, b)
        w1 = K.raw[:, slot, 0:CMP_ROW_TILES * SEQ].rearrange("p (r f) -> p r f", f=SEQ)
        for r in range(CMP_ROW_TILES):
            ins = nc.tensor.matmul(K.psum[0:M, 4 + kv, 0:SEQ], K.z2[:, kv, r, :], w1[:, r, :],
                                   start=r == 0, stop=r == CMP_ROW_TILES - 1)
        ins.then_inc(K.sem.slots_used, 1)
    pe.wait_ge(K.sem.slots_used, K.fills[b["fill0"] + b["w1_fill"] + 1][1] + 1)
    pe.nop().then_inc(K.sem.chid_ps, 1)
    pe.wait_ge(K.sem.gelu, 1)
    for kv in range(2):
        for j in range(2):
            o = (2 * kv + j) * M
            ins = nc.tensor.transpose(K.psum[:, 6, o:o + M], K.chid[0:M, kv, j * P:(j + 1) * P], K.ident[0:M, 0:M])
    ins.then_inc(K.sem.chidT_ps, 1)
    pe.wait_ge(K.sem.chidT, 1)
    for half in range(2):
        for j in range(2):
            nc.tensor.matmul(K.psum[half * HD:(half + 1) * HD, 7, 0:M], K.cw2[:, 0, j, :], K.chidT[:, 0, j, :],
                             start=j == 0, stop=j == 1)
    for g in range(G_B):
        for j in range(2):
            ins = nc.tensor.matmul(K.psum[0:N_CMP, 4, g * HD:(g + 1) * HD],
                                   K.chidT[:, 1, j, g * N_CMP:(g + 1) * N_CMP], K.cw2[:, 1, j, :],
                                   start=j == 0, stop=j == 1)
    ins.then_inc(K.sem.kcb_ps, 1)
    pe.wait_ge(K.sem.kcb, 1)
    for a in range(NT):
        for h in range(NH):
            g, hs = h // (NH // G_B), slice((h % 2) * HD, (h % 2 + 1) * HD)
            t = h // 2
            ins = nc.tensor.matmul(K.psum[:, CMP_BANKS[2 * a + h % 2], t * N_CMP:(t + 1) * N_CMP],
                                   K.qT[hs, t, a * P:(a + 1) * P],
                                   K.kcb[hs, g * N_CMP:(g + 1) * N_CMP], start=True, stop=True)
        ins.then_inc(K.sem.s_cmp, 1)


def pool_hybrid_loads(K, pool, b):
    nc, ins = K.nc, K.ins
    if b["n"]:
        pool.wait_ge(K.sem.y_done, NT * b["n"])
    nc.gpsimd.dma_start(K.c2[:, :], ins["consts"][:, C_FIRST:C_END]).then_inc(K.sem.h_rows, 16)
    nc.gpsimd.dma_start(K.bgrow[:, :], ins["b_gate_2"][0:1, :]).then_inc(K.sem.h_rows, 16)
    with nc.allow_non_contiguous_dma(reason="tables of a few thousand elements"):
        for t in range(CONV_T):
            nc.gpsimd.dma_start(K.cw[:, t, :], ins["conv_w_2"][0][:, t * P:(t + 1) * P].rearrange("k p -> p k"))\
                .then_inc(K.sem.h_small, 16)
        nc.gpsimd.dma_start(K.cbias[:, :], ins["conv_b_2"][0].rearrange("(t p) -> p t", p=P))\
            .then_inc(K.sem.h_small, 16)
    for dst, src in ((K.dtb[:, :], ins["dt_bias_2"]), (K.alog[:, :], ins["a_log_2"])):
        nc.gpsimd.dma_start(dst, src.rearrange("o r h -> o (r h)").to_broadcast([P, 2 * SSD_H]))\
            .then_inc(K.sem.h_small, 16)
    for dst, src, n in ((K.dskip[:, :], ins["d_skip_2"], SSD_H), (K.qkw[:, 0, :], ins["q_norm_w_2"], HD),
                        (K.qkw[:, 1, :], ins["k_norm_w_2"], HD), (K.ssdw[:, :], ins["ssd_norm_w_2"], SSD_W)):
        nc.gpsimd.dma_start(dst, src.to_broadcast([P, n])).then_inc(K.sem.h_small, 16)


H_SMALL = 16 * (CONV_T + 1 + 2 + 4)


def act_qk(K, act, b):
    nc = K.nc
    wait_projected(K, act, b)
    for a in range(NT):
        nc.scalar.activation(K.xs[:, a, 0:H_QK], K.qk[:, a, :], ACT.Square).then_inc(K.sem.h_sq, 1)
    g = K.gates[:, :, :].rearrange("p a n -> p (a n)")
    nc.scalar.activation(g, g, ACT.Sigmoid).then_inc(K.sem.h_zs, 1)
    z = K.z[:, :, :].rearrange("p a n -> p (a n)")
    nc.scalar.activation(z, z, ACT.Silu).then_inc(K.sem.h_zs, 1)
    act.wait_ge(K.sem.h_qk_ps, 1)
    nc.scalar.activation(K.qT[:, 0:4, :], K.psum[:, 4:6, :], ACT.Copy).then_inc(K.sem.h_qT, 1)


def dve_qk(K, dve, b):
    nc = K.nc

    def link(i):
        K.link(dve, "dve", i)

    wait_projected(K, dve, b)
    dve.wait_ge(K.sem.h_small, H_SMALL)
    dve.wait_ge(K.sem.h_rows, 32)
    dve.wait_ge(K.sem.h_sq, NT)
    ss, r = K.qkr[:, 0, :], K.qkr[:, 1, :]
    link(nc.vector.tensor_reduce(out=ss.rearrange("p (a h) -> p a h", a=NT),
                                 in_=K.xs[:, :, 0:H_QK].rearrange("p a (h d) -> p a h d", d=HD), axis=AX, op=ALU.add))
    dve_rstd(K, dve, r, ss, 1.0 / HD)
    qk = K.qk[:, :, :].rearrange("p a (h d) -> p (a h) d", d=HD)
    link(nc.vector.tensor_tensor(qk, qk, r.unsqueeze(2).to_broadcast([P, NT * 10, HD]), ALU.mult))
    for a in range(NT):
        q = K.qk[:, a, 0:H_Q].rearrange("p (h d) -> p h d", d=HD)
        k = K.qk[:, a, H_Q:].rearrange("p (h d) -> p h d", d=HD)
        link(nc.vector.tensor_tensor(q, q, K.qkw[:, 0, :].unsqueeze(1).to_broadcast([P, 8, HD]), ALU.mult))
        link(nc.vector.tensor_tensor(k, k, K.qkw[:, 1, :].unsqueeze(1).to_broadcast([P, 2, HD]), ALU.mult))
        cos = K.c2[:, C_COS - C_FIRST + a * HD:C_COS - C_FIRST + (a + 1) * HD]
        sin = K.c2[:, C_SIN - C_FIRST + a * HD:C_SIN - C_FIRST + (a + 1) * HD]
        x4 = K.qk[:, a, :].rearrange("p (h f u e) -> p (h f) u e", f=2, u=2, e=16)
        t4 = K.xs[:, a, 0:H_QK].rearrange("p (h f u e) -> p h f u e", f=2, u=2, e=16)
        s4 = sin.rearrange("p (f u e) -> p f u e", f=2, u=2)
        x5 = K.qk[:, a, :].rearrange("p (h f u e) -> p h f u e", f=2, u=2, e=16)
        for u in range(2):
            link(nc.vector.tensor_tensor(t4[:, :, :, u, :], x5[:, :, :, 1 - u, :],
                                         s4[:, :, u, :].unsqueeze(1).to_broadcast([P, 10, 2, 16]), ALU.mult))
        xa = K.qk[:, a, :].rearrange("p (h d) -> p h d", d=HD)
        link(nc.vector.tensor_tensor(xa, xa, cos.unsqueeze(1).to_broadcast([P, 10, HD]), ALU.mult))
        nc.vector.tensor_tensor(K.qk[:, a, :], K.qk[:, a, :], K.xs[:, a, 0:H_QK], ALU.add)\
            .then_inc(K.sem.h_rope, 1)
    dve.wait_ge(K.sem.h_qk_ps, 1)
    for g in range(2):
        for to in range(2):
            ins = nc.vector.tensor_copy(K.kT[to * HD:(to + 1) * HD, g, :], K.psum[g * HD:(g + 1) * HD, 6, 0:SEQ])
    ins.then_inc(K.sem.h_kT, 1)


def pe_qk(K, pe, b):
    wait_projected(K, pe, b)
    for a in range(NT):
        pe.wait_ge(K.sem.h_rope, a + 1)
        for t in range(5):
            o = (t % 2) * SEQ + a * P
            ins = K.nc.tensor.transpose(K.psum[:, 4 + t // 2, o:o + P], K.qk[:, a, t * P:(t + 1) * P], K.ident)
    ins.then_inc(K.sem.h_qk_ps, 1)


def pe_rows_product(K, pe, b, lhsT, fill, tiles, done):
    slot, landed = K.fill_of(b, fill)
    for j in range(3):
        pe.wait_ge(K.sem_raw[j], landed)
    w = K.raw[:, slot, 0:tiles * D].rearrange("p (r n) -> p r n", n=D)
    for a in range(NT):
        for half in range(2):
            for t in range(tiles):
                ins = K.nc.tensor.matmul(K.psum[:, 2 * a + half, :], lhsT[:, t, a * P:(a + 1) * P],
                                         w[:, t, half * 512:(half + 1) * 512], start=t == 0, stop=t == tiles - 1)
    ins.then_inc(K.sem.slots_used, 1)
    pe.wait_ge(K.sem.slots_used, K.fills[b["fill0"] + fill][1] + 1)
    pe.nop().then_inc(done, 1)


def y_tile(K, a):
    return K.psum[:, 2 * a:2 * a + 2, :].rearrange("p h n -> p (h n)")


TRI = C_TRI - C_FIRST


def tri(K, way, jt, i0=0, i1=SEQ):
    o = TRI + (way * NT + jt) * SEQ
    return K.c2[:, o + i0:o + i1]


def dve_conv(K, dve, b, taps):
    nc = K.nc
    if taps[0] == 0:
        K.link(dve, "dve", nc.vector.memset(K.xbc[:, :, 0:CONV_PAD], 0.0))
        K.link(dve, "dve", nc.vector.memset(K.xbc[:, :, SEQ + CONV_PAD:], 0.0))
    for k in taps:
        for t in range(CONV_T):
            src, acc, w = K.xbc[:, t, k:k + SEQ], K.xT[:, t, :], K.cw[:, t, k:k + 1]
            if k:
                dve.wait_ge(K.sem.h_conv, CONV_T * (k - 1) + t + 1)
                nc.vector.scalar_tensor_tensor(out=acc, in0=src, scalar=w, in1=acc, op0=ALU.mult, op1=ALU.add)\
                    .then_inc(K.sem.h_conv, 1)
            else:
                nc.vector.tensor_scalar(acc, src, w, None, ALU.mult).then_inc(K.sem.h_conv, 1)


def dve_ssd(K, dve, b):
    nc = K.nc

    def link(i):
        K.link(dve, "dve", i)

    dt = K.dt[:, :, :].rearrange("p a h -> p (a h)")
    e, sv, s2, p, q = (K.dts[:, i, :] for i in range(5))
    link(nc.vector.tensor_tensor(K.dt[:, :, :], K.dt[:, :, :],
                                 K.dtb[:, :].unsqueeze(1).to_broadcast([P, NT, 2 * SSD_H]), ALU.add))
    link(nc.vector.tensor_scalar(e, dt, -1.0, None, ALU.mult))
    nc.vector.tensor_tensor(e, e, dt, ALU.min).then_inc(K.sem.h_dtarg, 1)
    dve.wait_ge(K.sem.h_dtexp, 2)
    link(nc.vector.tensor_scalar(sv, e, 2.0, None, ALU.add))
    link(nc.vector.reciprocal(sv, sv))
    link(nc.vector.tensor_tensor(sv, sv, e, ALU.mult))
    link(nc.vector.tensor_tensor(s2, sv, sv, ALU.mult))
    link(nc.vector.tensor_scalar(p, s2, 1.0 / 17, None, ALU.mult))
    for k in range(7, 0, -1):
        link(nc.vector.scalar_tensor_tensor(out=p, in0=p, scalar=1.0 / (2 * k + 1), in1=s2, op0=ALU.add, op1=ALU.mult))
    link(nc.vector.scalar_tensor_tensor(out=p, in0=p, scalar=1.0, in1=sv, op0=ALU.add, op1=ALU.mult))
    link(nc.vector.tensor_scalar(dt, dt, 0.0, None, ALU.max))
    link(nc.vector.scalar_tensor_tensor(out=dt, in0=p, scalar=2.0, in1=dt, op0=ALU.mult, op1=ALU.add))
    nc.vector.scalar_tensor_tensor(out=K.dta[:, :, :], in0=K.dt[:, :, :], scalar=-1.0,
                                   in1=K.alog[:, :].unsqueeze(1).to_broadcast([P, NT, 2 * SSD_H]),
                                   op0=ALU.mult, op1=ALU.mult).then_inc(K.sem.h_dta, 1)
    dve.wait_ge(K.sem.h_ao, 1)
    dve.wait_ge(K.sem.h_zs, 2)
    for a in range(NT):
        nc.vector.tensor_tensor(K.xs[:, a, :], y_tile(K, a), K.gates[:, a, 0:D], ALU.mult)\
            .then_inc(K.sem.h_merge1, 1)
    dve.wait_ge(K.sem.h_acol_ps, 1)
    nc.vector.tensor_copy(K.acol[:, :, :].rearrange("p a h -> p (a h)"), K.psum[:, 0, 0:NT * 2 * SSD_H])
    dve.wait_ge(K.sem.h_cb_ps, 1)
    nc.vector.tensor_copy(K.cb[:, :, :, :].rearrange("p g j i -> p g (j i)"), K.psum[:, 1:3, :])
    dve.wait_ge(K.sem.h_xt_ps, 1)
    link(nc.vector.tensor_copy(K.xtok[:, :, :], K.psum[:, 6:8, :]))

    def args(h):
        dve.wait_ge(K.sem.h_row, h + 1)
        if h:
            dve.wait_ge(K.sem.h_w_sum, h)
        for n, (way, jt, i0, i1) in enumerate(SSD_PARTS):
            ins = nc.vector.tensor_scalar(K.dec[:, n, i0:i1], K.psum[:, 4 + h % 2, way * SEQ + i0:way * SEQ + i1],
                                          K.acol[:, jt, way * SSD_H + h:way * SSD_H + h + 1], 0.0,
                                          ALU.subtract, ALU.min)
        ins.then_inc(K.sem.h_arg, 1)

    def weights(h):
        g = h // (SSD_H // 2)
        dve.wait_ge(K.sem.h_exp, h + 1)
        for n, (way, jt, i0, i1) in enumerate(SSD_PARTS):
            ins = nc.vector.scalar_tensor_tensor(out=K.wgt[:, n, i0:i1], in0=K.dec[:, n, i0:i1],
                                                 scalar=K.dt[:, jt, way * SSD_H + h:way * SSD_H + h + 1],
                                                 in1=tri(K, way, jt, i0, i1), op0=ALU.mult, op1=ALU.mult)
        link(ins)
        nc.vector.tensor_tensor(K.wgt[:, 0, 0:P], K.wgt[:, 0, 0:P], K.wgt[:, 1, 0:P], ALU.add)
        K.link(dve, "dve", nc.vector.tensor_tensor(K.wgt[:, 3, P:], K.wgt[:, 3, P:], K.wgt[:, 2, P:], ALU.add))
        if h >= 2:
            dve.wait_ge(K.sem.h_y, h - 1)
        nc.vector.tensor_tensor(K.mm[:, h % 2, 0, :], K.wgt[:, 0, :], K.cb[:, g, 0, :], ALU.mult)
        nc.vector.tensor_tensor(K.mm[:, h % 2, 1, :], K.wgt[:, 3, :], K.cb[:, g, 1, :], ALU.mult)\
            .then_inc(K.sem.h_w_sum, 1)

    for h in range(SSD_H):
        args(h)
        weights(h)
    for a in range(NT):
        ya = K.ysd[:, a, :]
        y3 = ya.rearrange("p (h d) -> p h d", d=HD)
        link(nc.vector.tensor_tensor(y3, K.xtok[:, a, :].rearrange("p (h d) -> p h d", d=HD),
                                     K.dskip[:, :].unsqueeze(2).to_broadcast([P, SSD_H, HD]), ALU.mult))
        dve.wait_ge(K.sem.h_y, SSD_H)
        link(nc.vector.tensor_tensor(ya, ya, K.psum[:, 6 + a, :], ALU.add))
        nc.vector.tensor_tensor(ya, ya, K.z[:, a, :], ALU.mult).then_inc(K.sem.h_yss, 1)
        dve.wait_ge(K.sem.h_yn, a + 1)
        dve_rstd(K, dve, K.st[:, 10 + a:11 + a], K.st[:, 8 + a:9 + a], 1.0 / SSD_W)
        nc.vector.scalar_tensor_tensor(out=ya, in0=ya, scalar=K.st[:, 10 + a:11 + a], in1=K.ssdw[:, :],
                                       op0=ALU.mult, op1=ALU.mult).then_inc(K.sem.h_yT, 1)
    dve.wait_ge(K.sem.h_yT_ps, 1)
    nc.vector.tensor_copy(K.ssdT[:, :, :].rearrange("p t s -> p (t s)"),
                          K.psum[:, 4:6, :].rearrange("p b s -> p (b s)")).then_inc(K.sem.h_mT, 1)
    dve.wait_ge(K.sem.h_so, 1)
    for a in range(NT):
        link(nc.vector.tensor_tensor(K.gates[:, a, D:], y_tile(K, a), K.gates[:, a, D:], ALU.mult))
        nc.vector.tensor_tensor(K.xs[:, a, :], K.xs[:, a, :], K.gates[:, a, D:], ALU.add).then_inc(K.sem.h_merge2, 1)
    dve.wait_ge(K.sem.h_mT_ps, 1)
    nc.vector.tensor_copy(K.hT[:, 4:8, :].rearrange("p t s -> p (t s)"),
                          K.psum[:, 6:8, :].rearrange("p b s -> p (b s)")).then_inc(K.sem.h_mT, 1)


SSD_PARTS = ((0, 0, 0, SEQ), (1, 0, 0, P), (0, 1, P, SEQ), (1, 1, 0, SEQ))


def act_ssd(K, act, b):
    nc = K.nc
    for t in range(CONV_T):
        act.wait_ge(K.sem.h_conv, CONV_T * (CONV_K - 1) + t + 1)
        nc.scalar.activation(K.xT[:, t, :], K.xT[:, t, :], ACT.Silu, bias=K.cbias[:, t:t + 1])\
            .then_inc(K.sem.h_silu, 1)
    act.wait_ge(K.sem.h_dtarg, 1)
    nc.scalar.activation(K.dts[:, 0, :], K.dts[:, 0, :], ACT.Exp).then_inc(K.sem.h_dtexp, 1)
    nc.scalar.activation(K.alog[:, :], K.alog[:, :], ACT.Exp).then_inc(K.sem.h_dtexp, 1)
    for h in range(SSD_H):
        act.wait_ge(K.sem.h_arg, h + 1)
        for n, (way, jt, i0, i1) in enumerate(SSD_PARTS):
            ins = nc.scalar.activation(K.dec[:, n, i0:i1], K.dec[:, n, i0:i1], ACT.Exp)
        ins.then_inc(K.sem.h_exp, 1)
    for a in range(NT):
        act.wait_ge(K.sem.h_yss, a + 1)
        nc.scalar.activation(K.wgt[:, 2 * a:2 * a + 2, :].rearrange("p n s -> p (n s)"), K.ysd[:, a, :],
                             ACT.Square, accum_out=K.st[:, 8 + a:9 + a]).then_inc(K.sem.h_yn, 1)
    act.wait_ge(K.sem.h_mT_ps, 1)
    nc.scalar.activation(K.hT[:, 0:4, :].rearrange("p t s -> p (t s)"),
                         K.psum[:, 4:6, :].rearrange("p b s -> p (b s)"), ACT.Copy).then_inc(K.sem.h_qT, 1)


def pe_ssd(K, pe, b):
    nc = K.nc
    pe.wait_ge(K.sem.oT_sb, b["out0"] + NT * len(b["attn"].quads))
    pe_rows_product(K, pe, b, K.oT, b["ao_fill"], 4, K.sem.h_ao)
    pe.wait_ge(K.sem.h_merge1, NT)
    pe.wait_ge(K.sem.h_dta, 1)
    for jt in range(NT):
        for way in range(2):
            for k in range(NT):
                o = jt * 2 * SSD_H + way * SSD_H
                ins = nc.tensor.matmul(K.psum[:, 0, o:o + SSD_H], tri(K, way, k, jt * P, (jt + 1) * P),
                                       K.dta[:, k, way * SSD_H:(way + 1) * SSD_H], start=k == 0, stop=k == NT - 1)
    ins.then_inc(K.sem.h_acol_ps, 1)
    pe.wait_ge(K.sem.h_silu, CONV_T)
    for jt in range(NT):
        for g in range(2):
            hs = slice(g * HD, (g + 1) * HD)
            ins = nc.tensor.matmul(K.psum[:, 1 + g, jt * SEQ:(jt + 1) * SEQ], K.xT[hs, 4, jt * P:(jt + 1) * P],
                                   K.xT[hs, 5, :], start=True, stop=True)
    ins.then_inc(K.sem.h_cb_ps, 1)
    for a in range(NT):
        for t in range(4):
            ins = nc.tensor.transpose(K.psum[:, 6 + a, t * P:(t + 1) * P], K.xT[:, t, a * P:(a + 1) * P], K.ident)
    ins.then_inc(K.sem.h_xt_ps, 1)

    def rows(h):
        if h >= 2:
            pe.wait_ge(K.sem.h_arg, h - 1)
        for way in range(2):
            for k in range(NT):
                ins = nc.tensor.matmul(K.psum[:, 4 + h % 2, way * SEQ:(way + 1) * SEQ],
                                       K.dta[:, k, way * SSD_H + h:way * SSD_H + h + 1].to_broadcast([P, P]),
                                       tri(K, way, k), start=k == 0, stop=k == NT - 1)
        ins.then_inc(K.sem.h_row, 1)

    rows(0)
    for h in range(SSD_H):
        if h + 1 < SSD_H:
            rows(h + 1)
        pe.wait_ge(K.sem.h_w_sum, h + 1)
        for a in range(NT):
            for jt in range(NT):
                ins = nc.tensor.matmul(K.psum[:, 6 + a, h * HD:(h + 1) * HD], K.mm[:, h % 2, jt, a * P:(a + 1) * P],
                                       K.xtok[:, jt, h * HD:(h + 1) * HD], start=jt == 0, stop=jt == NT - 1)
        ins.then_inc(K.sem.h_y, 1)
    for a in range(NT):
        pe.wait_ge(K.sem.h_yT, a + 1)
        for t in range(4):
            o = (t % 2) * SEQ + a * P
            ins = nc.tensor.transpose(K.psum[:, 4 + t // 2, o:o + P], K.ysd[:, a, t * P:(t + 1) * P], K.ident)
    ins.then_inc(K.sem.h_yT_ps, 1)
    pe.wait_ge(K.sem.h_mT, 1)
    pe_rows_product(K, pe, b, K.ssdT, b["so_fill"], 4, K.sem.h_so)
    for a in range(NT):
        pe.wait_ge(K.sem.h_merge2, a + 1)
        for k in range(KT):
            o = (k % 2) * SEQ + a * P
            ins = nc.tensor.transpose(K.psum[:, 4 + k // 2, o:o + P], K.xs[:, a, k * P:(k + 1) * P], K.ident)
    ins.then_inc(K.sem.h_mT_ps, 1)
    pe.wait_ge(K.sem.h_mT, 2)
    pe.wait_ge(K.sem.h_qT, 2)


E_BANKS = 4


def pool_router_loads(K, pool, b):
    nc, ins = K.nc, K.ins
    if b["n"]:
        pool.wait_ge(K.sem.y_done, NT * b["n"])
    nc.gpsimd.dma_start(K.rw[:, :, 0:4], ins["w_router_group_2"][0].rearrange("(k p) e -> p k e", p=P))\
        .then_inc(K.sem.e_small, 16)
    nc.gpsimd.dma_start(K.rw[:, :, 4:20], ins["w_router_expert_2"][0].rearrange("(k p) e -> p k e", p=P))\
        .then_inc(K.sem.e_small, 16)
    nc.gpsimd.dma_start(K.rb[:, 0:4], ins["b_router_group_2"][0:1, :]).then_inc(K.sem.e_small, 16)
    nc.gpsimd.dma_start(K.rb[:, 4:20], ins["b_router_expert_2"][0:1, :]).then_inc(K.sem.e_small, 16)
    nc.gpsimd.dma_start(K.eidx[:, :], ins["consts"][:, C_IDX:C_END]).then_inc(K.sem.e_small, 16)


def dve_route(K, dve, b):
    nc = K.nc

    def link(i):
        K.link(dve, "dve", i)

    dve.wait_ge(K.sem.e_small, 80)
    for a in range(NT):
        ins = nc.vector.tensor_copy(K.hT[:, :, a * P:(a + 1) * P], turned(K, a, 0, KT))
    ins.then_inc(K.sem.e_hT, 1)
    dve.wait_ge(K.sem.e_lg, 1)
    link(nc.vector.tensor_copy(K.lg[:, :, :].rearrange("p a e -> p (a e)"), K.psum[:, 4, 0:NT * 20]))
    grp = K.lg[:, :, 0:4]
    fine = K.lg[:, :, 4:20].rearrange("p a (g e) -> p a g e", g=4)
    idx = K.eidx[:, 0:4].unsqueeze(1).to_broadcast([P, NT, 4])

    def four(i):
        return K.r4[:, i, :, :]

    def one(i):
        return K.r1[:, i, :]

    def wide(x):
        return x.unsqueeze(2).to_broadcast([P, NT, 4])

    def first_max(v, m, hot, tmp, t1):
        link(nc.vector.tensor_reduce(out=m, in_=v, axis=AX, op=ALU.max))
        link(nc.vector.tensor_tensor(tmp, v, wide(m), ALU.is_equal))
        link(nc.vector.tensor_tensor(tmp, tmp, idx, ALU.mult))
        link(nc.vector.tensor_reduce(out=t1, in_=tmp, axis=AX, op=ALU.max))
        link(nc.vector.tensor_tensor(hot, tmp, wide(t1), ALU.is_equal))

    gm, gsum, m1, m2, t1, gv, e2, r = (one(i) for i in range(8))
    goh, tmp, ge, fs, oh1, fs2, oh2, w = (four(i) for i in range(8))
    first_max(grp, gm, goh, tmp, t1)
    nc.vector.tensor_tensor(ge, grp, wide(gm), ALU.subtract).then_inc(K.sem.e_arg, 1)
    pr = K.p16[:, :, :].rearrange("p a (g e) -> p a g e", g=4)
    link(nc.vector.tensor_tensor(pr, fine, goh.unsqueeze(3).to_broadcast([P, NT, 4, 4]), ALU.mult))
    link(nc.vector.tensor_reduce(out=fs, in_=K.p16[:, :, :].rearrange("p a (g e) -> p a e g", g=4), axis=AX, op=ALU.add))
    first_max(fs, m1, oh1, tmp, t1)
    link(nc.vector.scalar_tensor_tensor(out=fs2, in0=oh1, scalar=NEG, in1=fs, op0=ALU.mult, op1=ALU.add))
    first_max(fs2, m2, oh2, tmp, t1)
    nc.vector.tensor_tensor(e2, m2, m1, ALU.subtract).then_inc(K.sem.e_arg, 1)
    dve.wait_ge(K.sem.e_exp, 2)
    link(nc.vector.tensor_reduce(out=gsum, in_=ge, axis=AX, op=ALU.add))
    link(nc.vector.reciprocal(gv, gsum))
    link(nc.vector.tensor_scalar(r, e2, 1.0, None, ALU.add))
    link(nc.vector.reciprocal(r, r))
    link(nc.vector.tensor_tensor(e2, e2, r, ALU.mult))
    link(nc.vector.tensor_tensor(oh1, oh1, wide(r), ALU.mult))
    link(nc.vector.tensor_tensor(oh2, oh2, wide(e2), ALU.mult))
    link(nc.vector.tensor_tensor(w, oh1, oh2, ALU.add))
    link(nc.vector.tensor_tensor(w, w, wide(gv), ALU.mult))
    for a in range(NT):
        ins = nc.vector.tensor_tensor(K.comb[:, a, :].rearrange("p (g e) -> p g e", g=4),
                                      K.r4[:, 0, a, :].unsqueeze(2).to_broadcast([P, 4, 4]),
                                      K.r4[:, 7, a, :].unsqueeze(1).to_broadcast([P, 4, 4]), ALU.mult)
    ins.then_inc(K.sem.e_comb, 1)
    for e in range(1, NEXP // 2, 2):
        dve.wait_ge(K.sem.e_rows, e + 1)
        nc.vector.tensor_copy(K.comb_bc[:, 2 * e:2 * e + 2, :].rearrange("p e s -> p (e s)"),
                              K.psum[:, 4 + e % E_BANKS, :]).then_inc(K.sem.comb, 1)
    dve.wait_ge(K.sem.e_act, NEXP // 4)
    dve.wait_ge(K.sem.comb, NEXP // 4)


def act_route(K, act, b):
    nc = K.nc
    act.wait_ge(K.sem.e_arg, 2)
    nc.scalar.activation(K.r4[:, 2, :, :], K.r4[:, 2, :, :], ACT.Exp).then_inc(K.sem.e_exp, 1)
    nc.scalar.activation(K.r1[:, 6, :], K.r1[:, 6, :], ACT.Exp).then_inc(K.sem.e_exp, 1)
    for e in range(0, NEXP // 2, 2):
        act.wait_ge(K.sem.e_rows, e + 1)
        nc.scalar.activation(K.comb_bc[:, 2 * e:2 * e + 2, :].rearrange("p e s -> p (e s)"),
                             K.psum[:, 4 + e % E_BANKS, :], ACT.Copy).then_inc(K.sem.e_act, 1)


def pe_route(K, pe, b):
    nc = K.nc
    pe.wait_ge(K.sem.e_small, 80)
    pe.wait_ge(K.sem.e_hT, 1)
    for a in range(NT):
        out = K.psum[:, 4, a * 20:(a + 1) * 20]
        nc.tensor.matmul(out, K.eidx[0:1, 4:4 + P], K.rb[0:1, :], start=True, stop=False)
        for k in range(KT):
            ins = nc.tensor.matmul(out, K.hT[:, k, a * P:(a + 1) * P], K.rw[:, k, :], start=False, stop=k == KT - 1)
    ins.then_inc(K.sem.e_lg, 1)
    pe.wait_ge(K.sem.e_comb, 1)
    for e in range(NEXP // 2):
        if e >= E_BANKS:
            pe.wait_ge(K.sem.e_act if e % 2 == 0 else K.sem.comb, (e - E_BANKS) // 2 + 1)
        for h in range(2):
            for a in range(NT):
                o = h * SEQ + a * P
                ins = nc.tensor.matmul(K.psum[:, 4 + e % E_BANKS, o:o + P],
                                       K.comb[:, a, 2 * e + h:2 * e + h + 1].to_broadcast([P, P]), K.ident,
                                       start=True, stop=True)
        ins.then_inc(K.sem.e_rows, 1)
    pe.wait_ge(K.sem.e_act, NEXP // 4)
    pe.wait_ge(K.sem.comb, NEXP // 4)


def sp_start(K, sp):
    sp.dma_start(K.x[:, :, :], K.ins["x"][0].rearrange("(a p) d -> p a d", p=P)).then_inc(K.sem.x_in, 16)
    sp.dma_start(K.cst[:, :], K.ins["consts"][:, 0:C_TOEPM]).then_inc(K.sem.consts_in, 16)


def act_start(K, act):
    if not K.uses_bias:
        return
    hot, msk = K.rows_hot, K.rows_mask
    act.dma_start(hot, K.ins["consts"][0:32, C_HOT:C_HOT + DTOEP]).then_inc(K.sem.bias_rows_in, 16)
    act.dma_start(msk, K.ins["consts"][0:NH, C_TOEPM:C_TOEPM + 2 * DTOEP]).then_inc(K.sem.bias_rows_in, 16)
    act.dma_start(K.rows_raw, K.ins["rel_bias"]).then_inc(K.sem.bias_rows_in, 16)
    act.dma_start(K.sink_raw[:, :], K.ins["a_sinks"].rearrange("(o j) h -> o (j h)", o=1).to_broadcast([P, 2 * NH]))\
        .then_inc(K.sem.sinks_in, 16)
    act.wait_ge(K.sem.bias_sum, 1)
    act.dma_start(K.scratch.rearrange("m h v -> h m v"), K.rows_sum).then_inc(K.sem.bias_rows_out, 16)
    act.wait_ge(K.sem.bias_rows_out, 16)
    act.dma_start(K.bias[:, :, :], bass.AP(K.scratch.tensor, 0, [[1, P], [DTOEP, NH], [1, SEQ]]))\
        .then_inc(K.sem.bias_in, 16)
    act.dma_start(K.biasA[:, :, :], bass.AP(K.scratch.tensor, NH * DTOEP,
                                            [[1, P], [DTOEP, NH], [1, P]])).then_inc(K.sem.bias_in, 16)


def pe_start(K, pe):
    if not K.uses_bias:
        return
    pe.wait_ge(K.sem.bias_rows_in, 48)
    pe.wait_ge(K.sem.bias_tab, 1)
    K.nc.tensor.matmul(K.psum[0:NH, 7, 0:DTOEP], K.rows_tab, K.rows_hot, start=True, stop=True)\
        .then_inc(K.sem.bias_ps, 1)


def dve_start(K, dve):
    if not K.uses_bias:
        return
    dve.wait_ge(K.sem.bias_rows_in, 48)
    K.nc.vector.tensor_copy(K.rows_tab.rearrange("p (q h t) -> p q h t", q=4, h=2),
                            K.rows_raw.rearrange("p (q t h) -> p q h t", q=4, h=2)).then_inc(K.sem.bias_tab, 1)
    dve.wait_ge(K.sem.sinks_in, 16)
    K.link(dve, "dve", K.nc.vector.tensor_copy(
        K.sink[:, :, :].rearrange("p j (q h t) -> p (j q) h t", q=4, h=2),
        K.sink_raw[:, :].rearrange("p (q t h) -> p q h t", q=8, h=2)))
    dve.wait_ge(K.sem.bias_ps, 1)
    row = K.psum[0:NH, 7, 0:DTOEP].unsqueeze(1).to_broadcast([NH, 2, DTOEP])
    K.nc.vector.tensor_tensor(K.rows_sum, row, K.rows_mask, ALU.add).then_inc(K.sem.bias_sum, 1)


def build(nc, ins, out, blocks):
    ctx = ExitStack()
    with ctx:
        K = Program(nc, ins, out, blocks, ctx)
        first_biased = next((b for b in blocks if b["kind"] in "ABC"), None)
        block = ctx.enter_context(nc.Block())

        @block.sync
        def _(sp):
            sp_start(K, sp)
            stream_weights(K, sp)
            store_x(K, sp)

        @block.scalar
        def _(act):
            act_start(K, act)
            for b in blocks:
                act_prenorm(K, act, b)
                if early_split(K, b):
                    act_first_splits(K, act, b, 1)
                act_hT(K, act, b)
                if b["kind"] == "moe":
                    act_route(K, act, b)
                if b["kind"] in ("ffn", "moe"):
                    act_ffn(K, act, b)
                else:
                    evacuate(K, act, b, 0)
                    if b is first_biased:
                        act_bias(K, act, b)
                    if b["kind"] == "B":
                        act_compress(K, act, b)
                    if b["kind"] == "H":
                        act_qk(K, act, b)
                    act_attention(K, act, b)
                    if b["kind"] == "H":
                        act_ssd(K, act, b)
                if b is not blocks[-1] and early_split(K, blocks[b["n"] + 1]):
                    act_first_splits(K, act, blocks[b["n"] + 1], 0)
                act_postnorm(K, act, b)

        @block.vector
        def _(dve):
            dve_start(K, dve)
            for b in blocks:
                dve_prenorm(K, dve, b)
                dve_hT(K, dve, b)
                if early_split(K, b):
                    dve_first_splits(K, dve, b, 1)
                if b["kind"] == "moe":
                    dve_route(K, dve, b)
                if b["kind"] in ("ffn", "moe"):
                    dve_ffn(K, dve, b)
                else:
                    evacuate(K, dve, b, 1)
                    if b["kind"] == "B":
                        dve_compress(K, dve, b)
                    if b["kind"] == "H":
                        dve_qk(K, dve, b)
                    dve_attention(K, dve, b)
                    if b["kind"] == "H":
                        dve_ssd(K, dve, b)
                if b is not blocks[-1] and early_split(K, blocks[b["n"] + 1]):
                    dve_first_splits(K, dve, blocks[b["n"] + 1], 0)
                dve_postnorm(K, dve, b)

        @block.gpsimd
        def _(pool):
            nc.gpsimd.dma_start(K.gain[0][:, :], K.gains[0].to_broadcast([P, D])).then_inc(K.sem_gain[0], 16)
            pool.wait_ge(K.sem.consts_in, 16)
            for b in blocks:
                pool_power(K, pool, b, "pre")
                pool_gains(K, pool, b)
                if b["kind"] == "moe":
                    pool_router_loads(K, pool, b)
                if b["kind"] in ("ffn", "moe"):
                    pool_ffn(K, pool, b)
                else:
                    if b["kind"] == "B":
                        pool_compress_loads(K, pool, b)
                    if b["kind"] == "H":
                        pool_hybrid_loads(K, pool, b)
                    pool_attention(K, pool, b)
                pool_power(K, pool, b, "post")

        @block.tensor
        def _(pe):
            pe_start(K, pe)
            for b in blocks:
                pe_transposes(K, pe, b)
                if b["kind"] == "moe":
                    pe_route(K, pe, b)
                if b["kind"] in ("ffn", "moe"):
                    pe_ffn(K, pe, b)
                else:
                    pe_projections(K, pe, b)
                    if b is first_biased:
                        pe_bias(K, pe, b)
                    if b["kind"] == "B":
                        pe_compress(K, pe, b)
                    if b["kind"] == "H":
                        pe_qk(K, pe, b)
                    pe_attention(K, pe, b)
                    if b["kind"] == "H":
                        pe_ssd(K, pe, b)
                    pe_output(K, pe, b)


_INS = ["x", "rel_bias", "norm_g", "ffn_w_in", "ffn_w_out", "a_w_in", "a_w_out", "a_sinks", "b_w_in", "b_w_out",
        "b_cmp_pos", "b_cmp_w1", "b_cmp_w2", "c_w_in", "c_w_out", "norm_mix_w_2", "w_in_2", "b_gate_2",
        "q_norm_w_2", "k_norm_w_2", "w_attn_o_2", "conv_w_2", "conv_b_2", "dt_bias_2", "a_log_2", "d_skip_2",
        "ssd_norm_w_2", "w_ssd_o_2", "w_out_2", "norm_ffn_w_2", "w_router_group_2", "b_router_group_2",
        "w_router_expert_2", "b_router_expert_2", "w1_2", "w3_2", "w2_2"]


def kernel(**inputs):
    import concourse.bacc as _bacc
    from concourse.bass_utils import run_bass_kernel_spmd as _run

    nc = _bacc.Bacc("TRN2", target_bir_lowering=False, num_devices=1)
    arrays, args = {}, {}
    for name in _INS:
        a = np.ascontiguousarray(inputs[name])
        arrays[f"in_{name}"] = a
        args[name] = nc.dram_tensor(f"in_{name}", a.shape, mybir.dt.from_np(a.dtype), kind="ExternalInput").ap()
    arrays["in_consts"] = make_consts()
    args["consts"] = nc.dram_tensor("in_consts", (P, C_END), F32, kind="ExternalInput").ap()
    out = nc.dram_tensor("out_0", (1, SEQ, D), F32, kind="ExternalOutput").ap()
    build(nc, args, out, block_list())
    r = _run(nc, [arrays], core_ids=[0])
    return r.results[0]["out_0"]
```
